# Optimizing a Trainium2 kernel written in Bass

```python
import math
import jax, jax.numpy as jnp
from jax import lax
import numpy as np
import jax
import jax.numpy as jnp

D_MODEL = 1024
BATCH = 1
SEQ = 256
DEPTH = 1

CTX_LEN = 256
GRID_W = 64
MIX_W = D_MODEL
F_W = MIX_W // 2
F_GROUPS = 4
F_GROUP_W = F_W // F_GROUPS
DN_W = MIX_W - F_W
DN_HEADS = 4
DK = DN_W // DN_HEADS
DV = DN_W // DN_HEADS
QK_W = DN_HEADS * DK
V_W = DN_HEADS * DV
CONV_CH = 2 * QK_W + V_W
W_IN = F_W + CONV_CH + V_W + 4 * DN_HEADS
CONV_K = 3
CHUNK = 64
N_GROUPS = 4
EXPERTS_PER_GROUP = 8
N_EXPERTS = N_GROUPS * EXPERTS_PER_GROUP
TOP_K = 2
D_EXPERT = D_MODEL // 2
MOE_BLOCK = 128
EPS = 1e-6


def rmsnorm(x, g):
    xf = x.astype(jnp.float32)
    y = xf * lax.rsqrt(jnp.mean(xf * xf, axis=-1, keepdims=True) + EPS) * g.astype(jnp.float32)
    return y.astype(x.dtype)

def l2norm(a):
    af = a.astype(jnp.float32)
    return af * lax.rsqrt(jnp.sum(af * af, axis=-1, keepdims=True) + EPS)

def modulate(h, shift, scale):
    return h * (1 + scale) + shift

def conv_grid(u, w):
    b, t, ch = u.shape
    rows = t // GRID_W
    y = lax.conv_general_dilated(u.reshape(b, rows, GRID_W, ch), w[:, :, None, :].astype(u.dtype),
                                 (1, 1), 'SAME', dimension_numbers=('NHWC', 'HWIO', 'NHWC'),
                                 feature_group_count=ch)
    return y.reshape(b, t, ch)

def conv_seq(u, w):
    ch = u.shape[-1]
    return lax.conv_general_dilated(u, w[1][:, None, :].astype(u.dtype), (1,), 'SAME',
                                    dimension_numbers=('NWC', 'WIO', 'NWC'), feature_group_count=ch)

def fourier_mix(f):
    b, t, _ = f.shape
    fg = f.astype(jnp.float32).reshape(b, t, F_GROUPS, F_GROUP_W)
    out = jnp.fft.fft2(fg, axes=(1, 3), norm='ortho').real
    return out.reshape(b, t, F_W).astype(f.dtype)

def gated_delta_chunked(q, k, v, g, beta, s0):
    b, t, h, dk = q.shape
    dv = v.shape[-1]
    n = t // CHUNK

    def chunks(a):
        a = jnp.moveaxis(a.astype(jnp.float32), 2, 1)
        return a.reshape(b, h, n, CHUNK, *a.shape[3:])

    q = chunks(q) * dk ** -0.5
    k = chunks(k)
    v = chunks(v)
    beta = chunks(beta)
    gc = jnp.cumsum(chunks(g), axis=-1)
    idx = jnp.arange(CHUNK)
    lower = idx[:, None] >= idx[None, :]
    decay = jnp.exp(jnp.where(lower, gc[..., :, None] - gc[..., None, :], -jnp.inf))
    k_beta = k * beta[..., None]
    m = jnp.where(idx[:, None] > idx[None, :],
                  jnp.einsum('bhnid,bhnjd->bhnij', k_beta, k) * decay, 0.0)
    eye = jnp.eye(CHUNK, dtype=jnp.float32)
    a_mat = eye + m
    t_inv = lax.linalg.triangular_solve(a_mat, jnp.broadcast_to(eye, a_mat.shape), left_side=True,
                                        lower=True, unit_diagonal=True)
    u = t_inv @ (v * beta[..., None])
    w = t_inv @ (k_beta * jnp.exp(gc)[..., None])
    intra = jnp.einsum('bhnid,bhnjd->bhnij', q, k) * decay

    def step(s, blk):
        q_i, k_i, u_i, w_i, a_i, g_i = blk
        v_new = u_i - w_i @ s
        o_i = (q_i * jnp.exp(g_i)[..., None]) @ s + a_i @ v_new
        g_last = g_i[..., -1:]
        s = s * jnp.exp(g_last)[..., None] + jnp.einsum(
            'bhcd,bhce->bhde', k_i * jnp.exp(g_last - g_i)[..., None], v_new)
        return s, o_i

    xs = tuple(jnp.moveaxis(a, 2, 0) for a in (q, k, u, w, intra, gc))
    s_final, o = lax.scan(step, s0.astype(jnp.float32), xs)
    o = jnp.moveaxis(o, 0, 2).reshape(b, h, t, dv)
    return jnp.moveaxis(o, 1, 2), s_final

def bidir_delta(q, k, v, g, beta, s0_fwd, s0_bwd):
    flip = lambda a: jnp.flip(a, axis=1)
    o_f, s_f = gated_delta_chunked(q, k, v, g[:, :, 0], beta[:, :, 0], s0_fwd)
    o_b, s_b = gated_delta_chunked(flip(q), flip(k), flip(v), flip(g[:, :, 1]), flip(beta[:, :, 1]), s0_bwd)
    return o_f + flip(o_b), s_f, s_b

def mixer_features(h, w_in, conv_w, a_log, dt_bias, conv_fn):
    b, t = h.shape[:2]
    p = h @ w_in
    f, qkv, z, gates = jnp.split(p, [F_W, F_W + CONV_CH, F_W + CONV_CH + V_W], axis=-1)
    qkv = jax.nn.silu(conv_fn(qkv, conv_w))
    q, k, v = jnp.split(qkv, [QK_W, 2 * QK_W], axis=-1)
    q = l2norm(q.reshape(b, t, DN_HEADS, DK))
    k = l2norm(k.reshape(b, t, DN_HEADS, DK))
    v = v.reshape(b, t, DN_HEADS, DV)
    gates = gates.astype(jnp.float32).reshape(b, t, 2, 2, DN_HEADS)
    beta = jax.nn.sigmoid(gates[:, :, 0])
    g = -jnp.exp(a_log.astype(jnp.float32)) * jax.nn.softplus(gates[:, :, 1] + dt_bias.astype(jnp.float32))
    return f, q, k, v, z, g, beta

def mixer_output(f, o, z, onorm_g, w_out):
    b, t = f.shape[:2]
    o = (rmsnorm(o, onorm_g) * jax.nn.silu(z.reshape(b, t, DN_HEADS, DV))).astype(f.dtype)
    return jnp.concatenate([fourier_mix(f), o.reshape(b, t, V_W)], axis=-1) @ w_out

def moe_ffn(h, w_group, b_group, w_router, b_router, w_gate, w_up, w_down):
    shp = h.shape
    d = shp[-1]
    xf = h.reshape(-1, d)
    n = xf.shape[0]
    pg = jax.nn.softmax((xf @ w_group).astype(jnp.float32) + b_group.astype(jnp.float32), axis=-1)
    pg_top, g_top = lax.top_k(pg, 1)
    el = ((xf @ w_router).astype(jnp.float32) + b_router.astype(jnp.float32)).reshape(
        n, N_GROUPS, EXPERTS_PER_GROUP)
    el_g = el[jnp.arange(n), g_top[:, 0]]
    pe_top, e_top = lax.top_k(jax.nn.softmax(el_g, axis=-1), TOP_K)
    wts = pg_top * pe_top / jnp.sum(pe_top, axis=-1, keepdims=True)
    eid = (g_top * EXPERTS_PER_GROUP + e_top).reshape(-1).astype(jnp.int32)
    w_f = wts.reshape(-1)
    n_assign = n * TOP_K
    order = jnp.argsort(eid)
    e_s = eid[order]
    tok_s = (order // TOP_K).astype(jnp.int32)
    w_s = w_f[order]
    counts = jnp.zeros((N_EXPERTS,), jnp.int32).at[eid].add(1)
    start = jnp.cumsum(counts) - counts
    pcounts = (counts + MOE_BLOCK - 1) // MOE_BLOCK * MOE_BLOCK
    pend = jnp.cumsum(pcounts)
    pstart = pend - pcounts
    dest = pstart[e_s] + (jnp.arange(n_assign, dtype=jnp.int32) - start[e_s])
    n_slots = -(-n_assign // MOE_BLOCK) * MOE_BLOCK + N_EXPERTS * MOE_BLOCK
    n_blocks = n_slots // MOE_BLOCK
    slot_tok = jnp.full((n_slots,), n, jnp.int32).at[dest].set(tok_s)
    slot_w = jnp.zeros((n_slots,), jnp.float32).at[dest].set(w_s)
    blk_expert = jnp.minimum(
        jnp.searchsorted(pend, jnp.arange(n_blocks, dtype=jnp.int32) * MOE_BLOCK, side='right'),
        N_EXPERTS - 1)
    x_pad = jnp.concatenate([xf, jnp.zeros((1, d), xf.dtype)], axis=0)
    xs = x_pad[slot_tok].reshape(n_blocks, MOE_BLOCK, d)

    def expert_block(args):
        xb, e = args
        hid = jax.nn.silu(xb @ w_gate[e]) * (xb @ w_up[e])
        return hid @ w_down[e]

    ys = lax.map(expert_block, (xs, blk_expert)).reshape(n_slots, d)
    out = jnp.zeros((n + 1, d), ys.dtype).at[slot_tok].add(ys * slot_w[:, None].astype(ys.dtype))
    return out[:n].reshape(shp)

def trunk_layer(x, ctx, c, c_ctx, w_mod, b_mod, norm1_g, w_in, conv_w, a_log, dt_bias, onorm_g, w_out,
                norm2_g, w_group, b_group, w_router, b_router, w_gate, w_up, w_down, update_ctx):
    mod_x = jnp.split((jax.nn.silu(c) @ w_mod + b_mod)[:, None, :], 6, axis=-1)
    mod_c = jnp.split((jax.nn.silu(c_ctx) @ w_mod + b_mod)[None, None, :], 6, axis=-1)

    hc = modulate(rmsnorm(ctx, norm1_g), mod_c[0], mod_c[1])
    fc, qc, kc, vc, zc, gc, bc = mixer_features(hc, w_in, conv_w, a_log, dt_bias, conv_seq)
    zero_state = jnp.zeros((ctx.shape[0], DN_HEADS, DK, DV), jnp.float32)
    oc, s_fwd, s_bwd = bidir_delta(qc, kc, vc, gc, bc, zero_state, zero_state)

    hx = modulate(rmsnorm(x, norm1_g), mod_x[0], mod_x[1])
    fx, qx, kx, vx, zx, gx, bx = mixer_features(hx, w_in, conv_w, a_log, dt_bias, conv_grid)
    ox, _, _ = bidir_delta(qx, kx, vx, gx, bx, s_fwd, s_bwd)
    x = x + mod_x[2] * mixer_output(fx, ox, zx, onorm_g, w_out)
    x = x + mod_x[5] * moe_ffn(modulate(rmsnorm(x, norm2_g), mod_x[3], mod_x[4]),
                               w_group, b_group, w_router, b_router, w_gate, w_up, w_down)
    if update_ctx:
        ctx = ctx + mod_c[2] * mixer_output(fc, oc, zc, onorm_g, w_out)
        ctx = ctx + mod_c[5] * moe_ffn(modulate(rmsnorm(ctx, norm2_g), mod_c[3], mod_c[4]),
                                       w_group, b_group, w_router, b_router, w_gate, w_up, w_down)
    return x, ctx

def first_inputs(seed: int = 0) -> dict:
    key = jax.random.key(seed)
    ks = jax.random.split(key, 24)
    nrm = lambda k, shape, s: jax.random.normal(k, shape, jnp.float32) * s
    x = nrm(ks[0], (BATCH, SEQ, D_MODEL), 1.0)
    c = nrm(ks[1], (BATCH, D_MODEL), 1.0)
    ctx = nrm(ks[2], (BATCH, CTX_LEN, D_MODEL), 1.0)
    c_ctx = nrm(ks[3], (D_MODEL,), 1.0)
    w_mod = nrm(ks[4], (DEPTH, D_MODEL, 6 * D_MODEL), 0.5 * D_MODEL ** -0.5)
    b_mod = nrm(ks[5], (DEPTH, 6 * D_MODEL), 0.01)
    norm1_g = 1.0 + nrm(ks[6], (DEPTH, D_MODEL), 0.02)
    w_in = nrm(ks[7], (DEPTH, D_MODEL, W_IN), D_MODEL ** -0.5)
    conv_w = nrm(ks[8], (DEPTH, CONV_K, CONV_K, CONV_CH), 1.0 / CONV_K)
    a_log = jnp.log(jax.random.uniform(ks[9], (DEPTH, 2, DN_HEADS), jnp.float32, 1.0, 16.0))
    dt = jnp.exp(jax.random.uniform(ks[10], (DEPTH, 2, DN_HEADS), jnp.float32,
                                    math.log(1e-3), math.log(1e-1)))
    dt_bias = dt + jnp.log(-jnp.expm1(-dt))
    onorm_g = 1.0 + nrm(ks[11], (DEPTH, DV), 0.02)
    w_out = nrm(ks[12], (DEPTH, MIX_W, D_MODEL), MIX_W ** -0.5)
    norm2_g = 1.0 + nrm(ks[13], (DEPTH, D_MODEL), 0.02)
    w_group = nrm(ks[14], (DEPTH, D_MODEL, N_GROUPS), D_MODEL ** -0.5)
    b_group = nrm(ks[15], (DEPTH, N_GROUPS), 0.01)
    w_router = nrm(ks[16], (DEPTH, D_MODEL, N_EXPERTS), D_MODEL ** -0.5)
    b_router = nrm(ks[17], (DEPTH, N_EXPERTS), 0.01)
    w_gate = nrm(ks[18], (DEPTH, N_EXPERTS, D_MODEL, D_EXPERT), D_MODEL ** -0.5)
    w_up = nrm(ks[19], (DEPTH, N_EXPERTS, D_MODEL, D_EXPERT), D_MODEL ** -0.5)
    w_down = nrm(ks[20], (DEPTH, N_EXPERTS, D_EXPERT, D_MODEL), D_EXPERT ** -0.5)
    final_g = 1.0 + nrm(ks[21], (D_MODEL,), 0.02)
    return {"x": x, "c": c, "ctx": ctx, "c_ctx": c_ctx, "w_mod": w_mod, "b_mod": b_mod,
            "norm1_g": norm1_g, "w_in": w_in, "conv_w": conv_w, "a_log": a_log, "dt_bias": dt_bias,
            "onorm_g": onorm_g, "w_out": w_out, "norm2_g": norm2_g, "w_group": w_group,
            "b_group": b_group, "w_router": w_router, "b_router": b_router, "w_gate": w_gate,
            "w_up": w_up, "w_down": w_down, "final_g": final_g}

def first_block(x, c, ctx, c_ctx, w_mod, b_mod, norm1_g, w_in, conv_w, a_log, dt_bias, onorm_g, w_out,
              norm2_g, w_group, b_group, w_router, b_router, w_gate, w_up, w_down, final_g):
    for l in range(DEPTH):
        x, ctx = trunk_layer(x, ctx, c, c_ctx, w_mod[l], b_mod[l], norm1_g[l], w_in[l], conv_w[l], a_log[l],
                             dt_bias[l], onorm_g[l], w_out[l], norm2_g[l], w_group[l], b_group[l],
                             w_router[l], b_router[l], w_gate[l], w_up[l], w_down[l],
                             update_ctx=(l < DEPTH - 1))
    return rmsnorm(x, final_g)


DEPTH_2 = 2

N_MEM = 256
ROPE_THETA = 500000.0
Q_BLOCK = 128

MLA_HEADS = 8
MLA_NOPE = 64
MLA_ROPE = 32
MLA_V = 64
MLA_Q_LORA = 384
MLA_KV_LORA = 256

SGU_GROUPS = 4
SGU_GROUP_DIM = 64
SGU_WIDTH = SGU_GROUPS * SGU_GROUP_DIM
SGU_CHUNK = 128

DIFF_HEADS = 4
DIFF_QK_DIM = 32
DIFF_V_DIM = 2 * DIFF_QK_DIM
DIFF_ROT = (2 * DIFF_QK_DIM) // 4 // 2

MIX_WIDTH = MLA_HEADS * MLA_V + SGU_WIDTH + DIFF_HEADS * DIFF_V_DIM

P_CQ = MLA_Q_LORA
P_CKV = MLA_KV_LORA
P_KR = MLA_ROPE
P_SGU = 2 * SGU_WIDTH
P_DQ = DIFF_HEADS * 2 * DIFF_QK_DIM
P_DK = DIFF_HEADS * 2 * DIFF_QK_DIM
P_DV = DIFF_HEADS * DIFF_V_DIM
IN_WIDTH = P_CQ + P_CKV + P_KR + P_SGU + P_DQ + P_DK + P_DV
IN_SPLIT = (P_CQ, P_CQ + P_CKV, P_CQ + P_CKV + P_KR, P_CQ + P_CKV + P_KR + P_SGU,
            P_CQ + P_CKV + P_KR + P_SGU + P_DQ, P_CQ + P_CKV + P_KR + P_SGU + P_DQ + P_DK)

X_HEADS = 4
X_HEAD_DIM = D_MODEL // X_HEADS

D_FF = 2816
CONV_WIDTH = 3


def rms_norm(x, g):
    xf = x.astype(jnp.float32)
    y = xf * lax.rsqrt(jnp.mean(xf * xf, axis=-1, keepdims=True) + EPS)
    return (y * g.astype(jnp.float32)).astype(x.dtype)

def layer_norm(x, g):
    xf = x.astype(jnp.float32)
    mu = jnp.mean(xf, axis=-1, keepdims=True)
    xc = xf - mu
    y = xc * lax.rsqrt(jnp.mean(xc * xc, axis=-1, keepdims=True) + EPS)
    return (y * g.astype(jnp.float32)).astype(x.dtype)

def rope_tables(positions, rot_dim):
    inv_freq = ROPE_THETA ** (-jnp.arange(0, rot_dim, 2, dtype=jnp.float32) / rot_dim)
    ang = positions.astype(jnp.float32)[..., None] * inv_freq
    return jnp.cos(ang), jnp.sin(ang)

def apply_rope(x, cos, sin):
    bshape = cos.shape[:2] + (1,) * (x.ndim - 3) + cos.shape[-1:]
    c = cos.reshape(bshape)
    s = sin.reshape(bshape)
    xf = x.astype(jnp.float32)
    x1, x2 = jnp.split(xf, 2, axis=-1)
    return jnp.concatenate([x1 * c - x2 * s, x2 * c + x1 * s], axis=-1).astype(x.dtype)

def partial_rope(x, cos, sin, rot):
    return jnp.concatenate([apply_rope(x[..., :rot], cos, sin), x[..., rot:]], axis=-1)

def to_query_blocks(q):
    b, s = q.shape[:2]
    return jnp.moveaxis(q.reshape((b, s // Q_BLOCK, Q_BLOCK) + q.shape[2:]), 1, 0)

def from_query_blocks(o):
    nb, b, qb = o.shape[:3]
    return jnp.moveaxis(o, 0, 1).reshape((b, nb * qb) + o.shape[3:])

def blocked_attention(q, k, v, scale):
    def block(qb):
        s = jnp.einsum('bqhd,bkhd->bhqk', qb, k).astype(jnp.float32) * scale
        p = jax.nn.softmax(s, axis=-1).astype(v.dtype)
        return jnp.einsum('bhqk,bkhd->bqhd', p, v)
    return from_query_blocks(lax.map(block, to_query_blocks(q)))

def mla_group(cq, ckv, kr, g_cq, g_ckv, w_uq, w_ukv, cos, sin):
    b, s, _ = cq.shape
    q = (rms_norm(cq, g_cq) @ w_uq).reshape(b, s, MLA_HEADS, MLA_NOPE + MLA_ROPE)
    q = jnp.concatenate([q[..., :MLA_NOPE], apply_rope(q[..., MLA_NOPE:], cos, sin)], axis=-1)
    kv = (rms_norm(ckv, g_ckv) @ w_ukv).reshape(b, s, MLA_HEADS, MLA_NOPE + MLA_V)
    k_nope, v = kv[..., :MLA_NOPE], kv[..., MLA_NOPE:]
    k_rope = apply_rope(kr[:, :, None, :], cos, sin)
    k = jnp.concatenate([k_nope, jnp.broadcast_to(k_rope, (b, s, MLA_HEADS, MLA_ROPE))], axis=-1)
    o = blocked_attention(q, k, v, (MLA_NOPE + MLA_ROPE) ** -0.5)
    return o.reshape(b, s, MLA_HEADS * MLA_V)

def sgu_group(z, g_sgu, w_s, b_s):
    b, s, _ = z.shape
    nc = s // SGU_CHUNK
    z = jax.nn.gelu(z, approximate=True)
    u, v = jnp.split(z, 2, axis=-1)
    u = u.reshape(b, nc, SGU_CHUNK, SGU_GROUPS, SGU_GROUP_DIM)
    v = layer_norm(v.reshape(b, nc, SGU_CHUNK, SGU_GROUPS, SGU_GROUP_DIM), g_sgu)
    mixed = jnp.einsum('gts,bnsgc->bntgc', w_s, v) + b_s.T[:, :, None]
    return (u * mixed).reshape(b, s, SGU_WIDTH)

def diff_group(dq, dk, dv, lam, lam_init, g_sub, cos, sin):
    b, s, _ = dq.shape
    q = partial_rope(dq.reshape(b, s, DIFF_HEADS, 2, DIFF_QK_DIM), cos, sin, 2 * DIFF_ROT)
    k = partial_rope(dk.reshape(b, s, DIFF_HEADS, 2, DIFF_QK_DIM), cos, sin, 2 * DIFF_ROT)
    v = dv.reshape(b, s, DIFF_HEADS, DIFF_V_DIM)
    scale = DIFF_QK_DIM ** -0.5

    def block(qb):
        sc = jnp.einsum('bqhcd,bkhcd->bhcqk', qb, k).astype(jnp.float32) * scale
        p = jax.nn.softmax(sc, axis=-1)
        a = (p[:, :, 0] - lam * p[:, :, 1]).astype(v.dtype)
        return jnp.einsum('bhqk,bkhe->bqhe', a, v)

    o = from_query_blocks(lax.map(block, to_query_blocks(q)))
    o = rms_norm(o, g_sub) * (1.0 - lam_init)
    return o.reshape(b, s, DIFF_HEADS * DIFF_V_DIM)

def memory_cross_attention(h, mem_n, w_q, w_kv, w_o):
    b, s, _ = h.shape
    m = mem_n.shape[1]
    q = (h @ w_q).reshape(b, s, X_HEADS, X_HEAD_DIM)
    kv = (mem_n @ w_kv).reshape(b, m, 2, X_HEADS, X_HEAD_DIM)
    k, v = kv[:, :, 0], kv[:, :, 1]
    sc = jnp.einsum('bqhd,bkhd->bhqk', q, k).astype(jnp.float32) * (X_HEAD_DIM ** -0.5)
    p = jax.nn.softmax(sc, axis=-1).astype(v.dtype)
    o = jnp.einsum('bhqk,bkhd->bqhd', p, v).reshape(b, s, D_MODEL)
    return o @ w_o

def conv_ffn(h, w_up, conv_w, conv_b, w_down):
    a = h @ w_up
    a = lax.conv_general_dilated(
        a, conv_w[:, None, :], window_strides=(1,),
        padding=((CONV_WIDTH // 2, CONV_WIDTH // 2),),
        dimension_numbers=('NWC', 'WIO', 'NWC'),
        feature_group_count=2 * D_FF) + conv_b
    g, u = jnp.split(a, 2, axis=-1)
    return (jax.nn.gelu(g, approximate=True) * u) @ w_down

def second_inputs(seed: int = 0) -> dict:
    key = jax.random.key(seed)
    ks = iter(jax.random.split(key, 40))

    def nrm(shape, scale):
        return jax.random.normal(next(ks), shape, jnp.float32) * scale

    def gain(dim_shape):
        return 1.0 + nrm((DEPTH_2,) + dim_shape, 0.05)

    x = nrm((BATCH, SEQ, D_MODEL), 1.0)
    mem = nrm((BATCH, N_MEM, D_MODEL), 1.0)
    offsets = jax.random.randint(next(ks), (BATCH, 1), 0, 4096, dtype=jnp.int32)
    positions = offsets + jnp.arange(SEQ, dtype=jnp.int32)[None, :]
    return {
        'x': x, 'mem': mem, 'positions': positions,
        'mix_pre_g': gain((D_MODEL,)),
        'mix_post_g': gain((D_MODEL,)),
        'w_in': nrm((DEPTH_2, D_MODEL, IN_WIDTH), D_MODEL ** -0.5),
        'mla_cq_g': gain((MLA_Q_LORA,)),
        'mla_ckv_g': gain((MLA_KV_LORA,)),
        'mla_w_uq': nrm((DEPTH_2, MLA_Q_LORA, MLA_HEADS * (MLA_NOPE + MLA_ROPE)), MLA_Q_LORA ** -0.5),
        'mla_w_ukv': nrm((DEPTH_2, MLA_KV_LORA, MLA_HEADS * (MLA_NOPE + MLA_V)), MLA_KV_LORA ** -0.5),
        'sgu_norm_g': gain((SGU_GROUPS, SGU_GROUP_DIM)),
        'sgu_w_s': nrm((DEPTH_2, SGU_GROUPS, SGU_CHUNK, SGU_CHUNK), SGU_CHUNK ** -0.5),
        'sgu_b_s': gain((SGU_GROUPS, SGU_CHUNK)),
        'diff_lam_q1': nrm((DEPTH_2, DIFF_QK_DIM), 0.1),
        'diff_lam_k1': nrm((DEPTH_2, DIFF_QK_DIM), 0.1),
        'diff_lam_q2': nrm((DEPTH_2, DIFF_QK_DIM), 0.1),
        'diff_lam_k2': nrm((DEPTH_2, DIFF_QK_DIM), 0.1),
        'diff_sub_g': gain((DIFF_V_DIM,)),
        'w_mix_out': nrm((DEPTH_2, MIX_WIDTH, D_MODEL), MIX_WIDTH ** -0.5),
        'mem_pre_g': gain((D_MODEL,)),
        'mem_post_g': gain((D_MODEL,)),
        'mem_kv_g': gain((D_MODEL,)),
        'mem_w_q': nrm((DEPTH_2, D_MODEL, D_MODEL), D_MODEL ** -0.5),
        'mem_w_kv': nrm((DEPTH_2, D_MODEL, 2 * D_MODEL), D_MODEL ** -0.5),
        'mem_w_o': nrm((DEPTH_2, D_MODEL, D_MODEL), D_MODEL ** -0.5),
        'ffn_pre_g': gain((D_MODEL,)),
        'ffn_post_g': gain((D_MODEL,)),
        'ffn_w_up': nrm((DEPTH_2, D_MODEL, 2 * D_FF), D_MODEL ** -0.5),
        'ffn_conv_w': nrm((DEPTH_2, CONV_WIDTH, 2 * D_FF), CONV_WIDTH ** -0.5),
        'ffn_conv_b': nrm((DEPTH_2, 2 * D_FF), 0.01),
        'ffn_w_down': nrm((DEPTH_2, D_FF, D_MODEL), D_FF ** -0.5),
    }

def second_block(x, mem, positions,
              mix_pre_g, mix_post_g, w_in, mla_cq_g, mla_ckv_g, mla_w_uq, mla_w_ukv,
              sgu_norm_g, sgu_w_s, sgu_b_s,
              diff_lam_q1, diff_lam_k1, diff_lam_q2, diff_lam_k2, diff_sub_g, w_mix_out,
              mem_pre_g, mem_post_g, mem_kv_g, mem_w_q, mem_w_kv, mem_w_o,
              ffn_pre_g, ffn_post_g, ffn_w_up, ffn_conv_w, ffn_conv_b, ffn_w_down):
    cos_a, sin_a = rope_tables(positions, MLA_ROPE)
    cos_d, sin_d = rope_tables(positions, 2 * DIFF_ROT)
    f32 = jnp.float32
    for l in range(DEPTH_2):
        lam_init = 0.8 - 0.6 * math.exp(-0.3 * l)
        h = rms_norm(x, mix_pre_g[l])
        proj = h @ w_in[l]
        cq, ckv, kr, z, dq, dk, dv = jnp.split(proj, IN_SPLIT, axis=-1)
        out_a = mla_group(cq, ckv, kr, mla_cq_g[l], mla_ckv_g[l], mla_w_uq[l], mla_w_ukv[l], cos_a, sin_a)
        out_b = sgu_group(z, sgu_norm_g[l], sgu_w_s[l], sgu_b_s[l])
        lam = (jnp.exp(jnp.sum(diff_lam_q1[l].astype(f32) * diff_lam_k1[l].astype(f32)))
               - jnp.exp(jnp.sum(diff_lam_q2[l].astype(f32) * diff_lam_k2[l].astype(f32)))
               + lam_init)
        out_c = diff_group(dq, dk, dv, lam, lam_init, diff_sub_g[l], cos_d, sin_d)
        mix = jnp.concatenate([out_a, out_b, out_c], axis=-1) @ w_mix_out[l]
        x = x + rms_norm(mix, mix_post_g[l])
        h = rms_norm(x, mem_pre_g[l])
        mem_n = rms_norm(mem, mem_kv_g[l])
        x = x + rms_norm(memory_cross_attention(h, mem_n, mem_w_q[l], mem_w_kv[l], mem_w_o[l]), mem_post_g[l])
        h = rms_norm(x, ffn_pre_g[l])
        x = x + rms_norm(conv_ffn(h, ffn_w_up[l], ffn_conv_w[l], ffn_conv_b[l], ffn_w_down[l]), ffn_post_g[l])
    return x


def setup_inputs(seed=0):
    out = dict(first_inputs(seed))
    for name, value in second_inputs(seed + 1).items():
        if name != "x":
            out[name + "_2"] = value
    return out


def reference(
    x, c, ctx, c_ctx, w_mod, b_mod, norm1_g, w_in, conv_w, a_log, dt_bias, onorm_g, w_out,
    norm2_g, w_group, b_group, w_router, b_router, w_gate, w_up, w_down, final_g, mem_2,
    positions_2, mix_pre_g_2, mix_post_g_2, w_in_2, mla_cq_g_2, mla_ckv_g_2, mla_w_uq_2,
    mla_w_ukv_2, sgu_norm_g_2, sgu_w_s_2, sgu_b_s_2, diff_lam_q1_2, diff_lam_k1_2,
    diff_lam_q2_2, diff_lam_k2_2, diff_sub_g_2, w_mix_out_2, mem_pre_g_2, mem_post_g_2,
    mem_kv_g_2, mem_w_q_2, mem_w_kv_2, mem_w_o_2, ffn_pre_g_2, ffn_post_g_2, ffn_w_up_2,
    ffn_conv_w_2, ffn_conv_b_2, ffn_w_down_2,
):
    x = first_block(
        x, c, ctx, c_ctx, w_mod, b_mod, norm1_g, w_in, conv_w, a_log, dt_bias, onorm_g, w_out,
        norm2_g, w_group, b_group, w_router, b_router, w_gate, w_up, w_down, final_g,
    )
    return second_block(
        x, mem_2, positions_2, mix_pre_g_2, mix_post_g_2, w_in_2, mla_cq_g_2, mla_ckv_g_2,
        mla_w_uq_2, mla_w_ukv_2, sgu_norm_g_2, sgu_w_s_2, sgu_b_s_2, diff_lam_q1_2,
        diff_lam_k1_2, diff_lam_q2_2, diff_lam_k2_2, diff_sub_g_2, w_mix_out_2, mem_pre_g_2,
        mem_post_g_2, mem_kv_g_2, mem_w_q_2, mem_w_kv_2, mem_w_o_2, ffn_pre_g_2, ffn_post_g_2,
        ffn_w_up_2, ffn_conv_w_2, ffn_conv_b_2, ffn_w_down_2,
    )


_drawn_inputs = setup_inputs


def setup_inputs(seed=0):
    import zlib

    import numpy as np

    out = dict(_drawn_inputs(seed))
    spreads = {}
    factors = {'c_ctx': 3.241,
     'b_mod': 3.002,
     'norm1_g': 4.751,
     'onorm_g': 5.153,
     'norm2_g': 4.104,
     'b_group': 34.559,
     'b_router': 6.402,
     'mla_cq_g_2': 8.0,
     'mla_ckv_g_2': 4.325,
     'diff_lam_k1_2': 3.22,
     'diff_lam_k2_2': 3.563,
     'ffn_conv_b_2': 5.746,
     'sgu_norm_g_2': 3.955,
     'sgu_b_s_2': 4.087,
     'diff_sub_g_2': 3.681}
    for name, (base, spread) in spreads.items():
        noise = np.random.default_rng([zlib.crc32(name.encode()), seed]).standard_normal(out[name].shape)
        drawn = base * np.exp(spread * noise) if base else spread * noise
        out[name] = jnp.asarray(drawn.astype(out[name].dtype))
    for name, factor in factors.items():
        out[name] = (out[name] * factor).astype(out[name].dtype)
    return out
```

```python
from contextlib import ExitStack

import concourse.bass as bass
from concourse import mybir

F32 = mybir.dt.float32
I32 = mybir.dt.int32
ALU = mybir.AluOpType
ACT = mybir.ActivationFunctionType
AX = mybir.AxisListType

P = 128
D = 1024
T = 256
TT = T // P
KC = D // P
EPS = 1e-6
H1 = 4
NEXP, NGRP, EPG = 32, 4, 8
DFF = 2816
GRID_R, GRID_W = 4, 64
PW = GRID_W + 2
SLOT = 2048
SLOTS = 12
NEG = -1.0e30
LEVELS = [1, 2, 4, 8, 16, 32, 64]
MLA_H, MLA_D, MLA_R = 8, 96, 32
DIFF_H = 4
XH = 4
N_FREQ = 24
LAYERS = 2
FFN_PAIRS = DFF // 256

S_MOD, S_IN, S_OUT = 24, 10, 4
S_EXP = 6
S_PRE = S_MOD + S_IN + S_OUT
S_MOE = S_EXP * NEXP
S_LAYER = 8 + 2 + 1 + 4 + 4 + 8 + 4 + 3 * FFN_PAIRS
S_ALL = S_PRE + S_MOE + LAYERS * S_LAYER


def offsets(sizes):
    at, out = 0, {}
    for name, n in sizes:
        out[name] = (at, n)
        at += n
    return out, at


PAR_1 = [("norm1", KC), ("norm2", KC), ("final", KC), ("bmod", 6 * KC), ("c", 2 * KC), ("conv", 9 * 12),
         ("onorm", 1), ("wgates", KC * 16), ("wroute", KC * 36)]
PAR_L = [("mix_pre", KC), ("mix_post", KC), ("cq", 3), ("ckv", 2), ("mem_pre", KC), ("mem_post", KC),
         ("mem_kv", KC), ("ffn_pre", KC), ("ffn_post", KC), ("fconv", 3 * 44), ("fbias", 44), ("sgu_b", 4)]
PAR, N_PAR = offsets(PAR_1 + [(f"{n}{l}", k) for l in range(LAYERS) for n, k in PAR_L])
ROW_1 = [("alog", 8), ("dtb", 8), ("bgroup", 4), ("brouter", 32)]
ROW_L = [("sgu_g", 256), ("sub_g", 64), ("lam", 128)]
ROW, N_ROW = offsets(ROW_1 + [(f"{n}{l}", k) for l in range(LAYERS) for n, k in ROW_L])
CST, N_CST = offsets([("ident", P), ("ones", P), ("cum0", P), ("cum1", P), ("neg0", P), ("neg1", P),
                      ("lev0", P * len(LEVELS)), ("lev1", P * len(LEVELS)), ("dftc", 2 * P),
                      ("invf", N_FREQ), ("first4", 4), ("first8", 8)])


def constants():
    import numpy as np
    c = np.zeros((P, N_CST), np.float32)

    def put(name, a):
        o, n = CST[name]
        c[:, o:o + n] = np.asarray(a, np.float64).reshape(P, n)

    i, j = np.arange(P)[None, :], np.arange(P)[:, None]
    put("ident", i == j)
    put("ones", np.ones((P, P)))
    put("cum0", j <= i)
    put("cum1", j >= i)
    put("neg0", np.where(j <= i, 0, NEG))
    put("neg1", np.where(j >= i, 0, NEG))
    lev = [-1.0 * ((j // (2 * s) == i // (2 * s)) & (j % (2 * s) < s) & (i % (2 * s) >= s)) for s in LEVELS]
    put("lev0", np.stack(lev, 1))
    put("lev1", np.stack([m.T for m in lev], 1))
    t = np.arange(T)
    ang = 2 * np.pi * ((t[:, None] * t[None, :]) % T) / T
    s = 1.0 / np.sqrt(T * P)
    dft = np.concatenate([np.cos(ang) * s, np.sin(ang) * s], 1).reshape(TT, P, 2 * T).transpose(1, 0, 2)
    t = np.arange(P)
    ang = 2 * np.pi * ((t[:, None] * t[None, :]) % P) / P
    put("dftc", np.concatenate([np.cos(ang), -np.sin(ang)], 1))
    f1 = np.float32(500000.0) ** (-np.arange(0, 32, 2, dtype=np.float32) / np.float32(32))
    f2 = np.float32(500000.0) ** (-np.arange(0, 16, 2, dtype=np.float32) / np.float32(16))
    put("invf", np.tile(np.concatenate([f1, f2]), (P, 1)))
    put("first4", np.tile(np.arange(4, 0, -1), (P, 1)))
    put("first8", np.tile(np.arange(8, 0, -1), (P, 1)))
    return c, np.ascontiguousarray(dft, np.float32)


def trunk_kernel(nc, stream, par_d, row_d, cst_d, dft_d, xc_d, mem_d, pos_d, sguw_d, out_d):
    ctx = ExitStack()
    with ctx:
        def sb(name, shape, dt=F32):
            return ctx.enter_context(nc.sbuf_tensor(name, shape, dt))

        def sem(name):
            return ctx.enter_context(nc.semaphore(name))

        ring = sb("ring", [P, SLOTS, SLOT])
        cst = sb("cst", [P, N_CST])
        par = sb("par", [P, N_PAR])
        row = sb("row", [P, N_ROW])
        xT = sb("xT", [P, KC, T])
        small = sb("small", [P, 1400])
        ipos = sb("ipos", [P, TT], I32)
        arena = sb("arena", [P, 19456])
        ps = ctx.enter_context(nc.psum_tensor("ps", [P, 8, 512], F32))

        def view(t, at, *dims):
            n = 1
            for d in dims:
                n *= d
            v = t[:, at:at + n]
            if len(dims) == 2:
                v = v.rearrange("p (a b) -> p a b", a=dims[0])
            elif len(dims) == 3:
                v = v.rearrange("p (a b c) -> p a b c", a=dims[0], b=dims[1])
            return v

        def C(name, *dims):
            o, n = CST[name]
            return view(cst, o, *(dims or (n,)))

        def PR(name, *dims):
            o, n = PAR[name]
            return view(par, o, *(dims or (n,)))

        def RW(name, *dims):
            o, n = ROW[name]
            return view(row, o, *(dims or (n,)))

        ident, ones = C("ident"), C("ones")
        sm_at = [0]

        def S(*dims):
            n = 1
            for d in dims:
                n *= d
            v = view(small, sm_at[0], *dims)
            sm_at[0] += n
            assert sm_at[0] <= 1400
            return v

        def bank(b, *dims):
            n = 1
            for d in dims:
                n *= d
            k = -(-n // 512)
            v = ps[:, b:b + k, :].rearrange("p a b -> p (a b)")[:, 0:n]
            if len(dims) == 2:
                v = v.rearrange("p (a b) -> p a b", a=dims[0])
            elif len(dims) == 3:
                v = v.rearrange("p (a b c) -> p a b c", a=dims[0], b=dims[1])
            return v

        def over(a, shape, axis=1):
            return a.unsqueeze(axis).to_broadcast(shape)

        def wA(s, c, half, kc=KC):
            n = SLOT // kc
            return ring[:, s % SLOTS, c * n + half * P:c * n + half * P + P]

        def wB(s, c, lo, n, kc=KC, width=None):
            w = width or SLOT // kc
            return ring[:, s % SLOTS, c * w + lo:c * w + lo + n]

        silu_c = S(KC, 2)
        mods = S(6 * KC, 2)
        mulx, mulc = S(KC), S(KC)
        mul2 = S(KC)
        beta = S(2, 4, H1)
        gt = S(2, 4, H1)
        gc = S(2, 4, H1)
        eg = S(2, 4, H1)
        ed = S(2, 4, H1)
        et = S(2, 4, H1)
        beg = S(2, 4, H1)
        gtmp, gtmp2 = S(4, 8), S(4, 8)
        nega = S(8)
        posf = S(TT)
        ang, angk, cosx, sinx = S(TT, N_FREQ), S(TT, N_FREQ), S(TT, N_FREQ), S(TT, N_FREQ)
        logits = S(TT, 36)
        r4a, r4b, r8a, r8b, r8c = S(TT, 4), S(TT, 4), S(TT, 8), S(TT, 8), S(TT, 8)
        elp = S(TT, 32)
        r1v = S(7, TT)
        comb = S(TT, 32)
        graw = S(4, 16)
        mx, nmx, rsum, rinv = S(2, 4), S(2, 4), S(2, 4), S(2, 4)
        lam_p, lam_s, nlam = S(2, 32), S(4), S(2)
        st8, st8b = S(8), S(8)

        def A(at, *dims):
            return view(arena, at, *dims)

        ctxT = A(0, KC, T)
        gate_w = PR("wgates", KC, 16)
        hA = A(2048, KC, 2 * T)
        sqA = A(6144, KC, 2 * T)
        rsA = A(10240, 2 * T)
        padx = A(6144, 12, (GRID_R + 2) * PW)
        padc = A(10896, 8, T + 2)
        vT = A(0, H1, 2 * T)
        qT = A(12960, H1, T)
        kT = A(13984, H1, 2 * T)
        zT = A(16032, H1, T)
        ft = A(17056, TT, 512)
        sqk, sqq = A(6144, H1, 2 * T), A(8192, H1, T)
        rsk, rsq = A(9216, H1, 2 * T), A(11264, H1, T)
        dftT = A(2048, TT, 2 * T)
        dftG = A(3072, 2, 2 * T)
        catF, oT = A(18080, H1, T), A(17056, H1, T)
        bM, bC, bD, bT, bU, bA, bQ, bS, bV = [A(2048 + 1024 * n, 2, H1, P) for n in range(9)]
        sqo = A(2048, H1, T)
        rso = A(3072, H1, T)
        h2 = A(0, KC, T)
        sq = A(2048, KC, T)
        rs = A(4096, 2 * T)
        wrow = A(4608, NEXP, T)
        diag = A(12800, 4, T)
        hid = A(14848, 4, T)
        sg = A(15872, 2, 2, T)
        h = h2
        memN = A(4608, KC, T)
        cat = A(6656, KC, T)
        yb = A(8704, KC, T)
        cv = A(8704, 5, T)
        krt = A(9984, TT, 32)
        zt = A(10048, TT, 512)
        dt_ = A(11072, TT, 768)
        qt = A(12608, TT, 768)
        kc = A(14144, TT, 768)
        vt = A(15680, TT, 512)
        QT, KT = A(0, MLA_H, T), A(2048, MLA_H, T)
        rtmp = A(16704, 4, TT * 8 * 16)
        rtk = A(17728, 4, TT * 16)
        Pb = [A(16704, TT, T), A(17216, TT, T), A(13120, TT, T), A(13632, TT, T)]
        PTb = [A(17728, TT, T), A(18240, TT, T)]
        ot = A(18752, TT, 256)
        dqT, dkT = A(8704, 2, T), A(9216, 2, T)
        ob = A(12608, TT, 256)
        sguw = A(14144, 4, P)
        xc2 = A(14656, TT, 256)
        memn = A(8704, KC, T)
        vm = A(10752, TT, D)
        qm = A(12800, KC, T)
        km = A(0, KC, T)
        ca = A(8704, 2, 4, T)
        fT = A(10752, 2, 2, T)

        ld_par, ld_x, ld_mem, ld_dft, ld_sgu, out_done = [sem(f"ld{i}") for i in range(6)]
        full = [sem(f"slot_full{i}") for i in range(SLOTS)]
        free = sem("slots_free")
        v_step, a_step, zeroed = sem("v_step"), sem("a_step"), sem("zeroed")
        sq_ok, ss_ps, h_ok, x_ok = sem("sq_ok"), sem("ss_ps"), sem("h_ok"), sem("x_ok")
        root_ok = sem("root_ok")
        silu_c_ok, mod_ps, mods_ok = sem("silu_c_ok"), sem("mod_ps"), sem("mods_ok")
        proj_ps, proj_ev = sem("proj_ps"), sem("proj_ev")
        conv_ok, act_ok = sem("conv_ok"), sem("act_ok")
        l2_sq, l2_ps, l2_ok = sem("l2_sq"), sem("l2_ps"), sem("l2_ok")
        gate_v, gate_a, gate_ps = sem("gate_v"), sem("gate_a"), sem("gate_ps")
        four_ps, four_g, four_cat = sem("four_ps"), sem("four_g"), sem("four_cat")
        gdn = {n: sem("gdn_" + n) for n in ("rows", "gb", "kk", "pre", "exp", "eq", "m", "ct", "u", "uc", "vv", "d",
                                            "tr", "tok", "nw", "nwc", "vn", "vnc", "st", "S")}
        o_sq, o_ps, o_ok = sem("o_sq"), sem("o_ps"), sem("o_ok")
        rt_ps, rt_v, rt_a, rt_w = sem("rt_ps"), sem("rt_v"), sem("rt_a"), sem("rt_w")
        dg_ok, wr_ps, wr_ok = sem("dg_ok"), sem("wr_ps"), sem("wr_ok")
        gu_ps, sg_ok, hid_ok, moe_ps = sem("gu_ps"), sem("sg_ok"), sem("hid_ok"), sem("moe_ps")
        up_w = sem("sg_up")
        rope_v, rope_a = sem("rope_v"), sem("rope_a")
        mem_sq, mem_ok = sem("mem_sq"), sem("mem_ok")
        qk_ok, tq_ps, tq_ev = sem("qk_ok"), sem("tq_ps"), sem("tq_ev")
        sc_ps, max_ok, exp_ok, p_ok, pt_ps, pt_ev, o2_ps, o2_ev = [
            sem("at_" + n) for n in ("sc", "max", "exp", "p", "pt", "ptev", "o", "oev")]
        ln_ok, mix_ps, ob_ok = sem("ln_ok"), sem("mix_ps"), sem("ob_ok")
        ot_ok, tc_ps, cat_ok = sem("ot_ok"), sem("tc_ps"), sem("cat_ok")
        memn_ok = sem("memn_ok")
        up_ps, tap_ok, conv2_ok, gelu_ok, f_ok, ffn_ps, y_ok = [
            sem("ffn_" + n) for n in ("up", "tap", "conv", "gelu", "f", "y", "yev")]

        block = ctx.enter_context(nc.Block())

        @block.sync
        def _(sp):
            for n in range(SLOTS):
                sp.dma_start(ring[:, n, :], stream[n]).then_inc(full[n], 16)
            with sp.Fori(0, S_ALL // SLOTS - 1) as r:
                for j in range(SLOTS):
                    sp.wait_ge(free, r * SLOTS + (j + 1))
                    sp.dma_start(ring[:, j, :], stream[r * SLOTS + (SLOTS + j)]).then_inc(full[j], 16)
            for n in range(S_ALL // SLOTS * SLOTS, S_ALL):
                sp.wait_ge(free, n - SLOTS + 1)
                sp.dma_start(ring[:, n % SLOTS, :], stream[n]).then_inc(full[n % SLOTS], 16)

        @block.gpsimd
        def _(pool):
            pool.wait_ge(h_ok, 1)
            nc.gpsimd.memset(arena[:, 6144:12960], 0.0).then_inc(zeroed, 1)

        def new_step(eng, step):
            n = [0]

            def link(ins):
                n[0] += 1
                ins.then_inc(step, 1)
                eng.wait_ge(step, n[0])
            return link

        def new_signal(eng):
            counts = {}

            def signal(ins, s, wait=True):
                counts[s.name] = counts.get(s.name, 0) + 1
                ins.then_inc(s, 1)
                if wait:
                    eng.wait_ge(s, counts[s.name])
                return counts[s.name]
            return signal

        @block.tensor
        def _(pe):
            pend = [0]
            pos = [0]
            jobs = [0]

            def mm(out, lhsT, rhs, start=True, stop=True, inc=None, tr=False, skip=False):
                if tr:
                    i = nc.tensor.transpose(out, lhsT, rhs)
                else:
                    i = nc.tensor.matmul(out, lhsT, rhs, start=start, stop=stop, skip_group_check=skip)
                if inc is not None:
                    i.then_inc(inc, 1)
                elif pend[0]:
                    i.then_inc(free, pend[0])
                    pend[0] = 0
                return i

            def arrive():
                n = pos[0]
                pe.wait_ge(full[n % SLOTS], 16 * (n // SLOTS + 1))
                pos[0] += 1
                return n

            def release():
                pend[0] += 1

            def job_bank():
                j = jobs[0]
                if j >= 4:
                    pe.wait_ge(proj_ev, j - 3)
                jobs[0] += 1
                return j % 4

            def job_a(s, half, mov, n, kc=KC):
                out = bank(job_bank(), n)
                for c in range(kc):
                    mm(out, wA(s, c, half, kc), mov[:, c, :], c == 0, c == kc - 1,
                       proj_ps if c == kc - 1 else None)

            def job_b(s, src, t0, lo, n, tiles=1, kc=KC, width=None):
                b = job_bank()
                for t in range(tiles):
                    for c in range(kc):
                        last = c == kc - 1
                        mm(bank(b, tiles * n)[:, t * n:t * n + n], src[:, c, t0 + t * P:t0 + t * P + P],
                           wB(s, c, lo, n, kc, width), c == 0, last, proj_ps if last and t == tiles - 1 else None)

            norms = [0]

            def sum_squares(parts, n):
                norms[0] += 1
                pe.wait_ge(sq_ok, norms[0])
                if norms[0] > 1:
                    pe.wait_ge(h_ok, norms[0] - 1)
                for k, (v, chunks) in enumerate(parts):
                    for i, c in enumerate(chunks):
                        last = i == len(chunks) - 1
                        mm(bank(4, len(parts) * n)[:, k * n:k * n + n], ones, v[:, c, :], i == 0, last,
                           ss_ps if last and k == len(parts) - 1 else None)

            pe.wait_ge(ld_par, 48)
            sum_squares([(sqA, range(KC))], 2 * T)
            pe.wait_ge(silu_c_ok, 1)
            with pe.Fori(0, S_MOD // SLOTS) as r:
                for j in range(SLOTS):
                    pe.wait_ge(full[j], r * 16 + 16)
                    for half in range(2):
                        for c in range(KC):
                            i = nc.tensor.matmul(ps[:, 5, bass.ds(r * (4 * SLOTS) + (4 * j + 2 * half), 2)],
                                                 wA(j, c, half), silu_c[:, c, :], start=c == 0, stop=c == KC - 1)
                    i.then_inc(free, 1)
            pos[0] = S_MOD
            mm(bank(6, 1), ident, ident[:, 0:1], inc=mod_ps)

            pe.wait_ge(h_ok, 1)
            b = job_bank()
            for t in range(4):
                for c in range(KC):
                    mm(bank(b, 4, 16)[:, t, :], hA[:, c, t * P:t * P + P], gate_w[:, c, :], c == 0, c == KC - 1,
                       proj_ps if c == KC - 1 and t == 3 else None)
            for k in range(2):
                s = arrive()
                for t in range(TT):
                    job_b(s, hA, T + t * P, 0, T)
                release()
            for k in range(8):
                s = arrive()
                for half in range(2):
                    job_a(s, half, hA[:, :, T:2 * T] if k < 2 or k >= 6 else hA, T if k < 2 or k >= 6 else 2 * T)
                release()

            pe.wait_ge(l2_sq, 2)
            pe.wait_ge(proj_ev, jobs[0])
            for hd in range(H1):
                mm(bank(hd, 2 * T), ones, sqk[:, hd, :])
            for hd in range(H1):
                mm(bank(4 + hd // 2, 2 * T)[:, hd % 2 * T:hd % 2 * T + T], ones, sqq[:, hd, :],
                   inc=l2_ps if hd == H1 - 1 else None)

            pe.wait_ge(gate_v, 2)
            gflat = gt.rearrange("p d t h -> p d (t h)")
            for d in range(2):
                mm(bank(6, 64)[:, 16 * d:16 * d + 16], C(f"cum{d}"), gflat[:, d, :])
            mm(bank(6, 64)[:, 32:64], ones, gt.rearrange("p d t h -> p (d t h)"), inc=gate_ps)

            pe.wait_ge(ld_dft, 16)
            pe.wait_ge(l2_ok, 1)
            for g in range(4):
                for t in range(TT):
                    mm(bank(g % 2, 2 * T), ft[:, t, g * P:g * P + P], dftT[:, t, :], t == 0, t == 1,
                       four_ps if t == 1 else None)
                pe.wait_ge(four_g, g + 1)
                if g >= 2:
                    pe.wait_ge(four_cat, g - 1)
                for k in range(2):
                    mm(bank(2 + g % 2, T), view(cst, CST["dftc"][0] + k * P, P), dftG[:, g % 2, k * T:k * T + T],
                       k == 0, k == 1, four_ps if k == 1 else None)

            for s in range(4):
                tiles = (s, s ^ 1)
                xs = s >= 2

                def heads(b, lhsT, rhs, sig=None):
                    for hd in range(H1):
                        mm(bank(b, H1, P)[:, hd, :], lhsT(hd), rhs(hd), inc=sig if hd == H1 - 1 else None)

                if s == 0:
                    pe.wait_ge(four_cat, 4)
                for d in range(2):
                    tk = slice(tiles[d] * P, tiles[d] * P + P)
                    tq = slice((tiles[d] - 2) * P, (tiles[d] - 2) * P + P)
                    pe.wait_ge(gdn["rows"], 2 * s + d + 1)
                    mm(bank(d, 512), ones, bD[:, d].rearrange("p h i -> p (h i)"))
                    mm(bank(2 + d, 512), ones, bU[:, d].rearrange("p h i -> p (h i)"), inc=gdn["gb"])
                    heads(4 + d, lambda hd: kT[:, hd, tk], lambda hd: kT[:, hd, tk], None if xs else gdn["kk"])
                    if xs:
                        heads(6 + d, lambda hd: kT[:, hd, tk], lambda hd: qT[:, hd, tq], gdn["kk"])
                for d in range(2):
                    pe.wait_ge(gdn["ct"], 14 * s + d + 1)
                    for hd in range(H1):
                        mm(bank(d, H1, P)[:, hd, :], bC[:, d, hd, :], ident, tr=True,
                           inc=gdn["u"] if hd == H1 - 1 else None)
                for v in range(1, len(LEVELS)):
                    for d in range(2):
                        pe.wait_ge(gdn["ct"], 14 * s + 2 * v + d + 1)
                        pe.wait_ge(gdn["d"], 14 * s + 2 * (v - 1) + d + 1)
                        heads(d, lambda hd: bC[:, d, hd, :], lambda hd: bD[:, d, hd, :], gdn["u"])
                    for d in range(2):
                        pe.wait_ge(gdn["uc"], 12 * s + 2 * (v - 1) + d + 1)
                        if v < len(LEVELS) - 1:
                            heads(2 + d, lambda hd: bT[:, d, hd, :], lambda hd: bU[:, d, hd, :])
                        heads(4 + d, lambda hd: bU[:, d, hd, :], lambda hd: bT[:, d, hd, :], gdn["vv"])
                for d in range(2):
                    for hd in range(H1):
                        mm(bank(d, H1, P)[:, hd, :], kT[:, hd, tiles[d] * P:tiles[d] * P + P], ident, tr=True)
                    for hd in range(H1):
                        mm(bank(6 + d, H1, P)[:, hd, :], vT[:, hd, tiles[d] * P:tiles[d] * P + P], ident, tr=True,
                           inc=gdn["tr"] if hd == H1 - 1 else None)
                for d in range(2):
                    pe.wait_ge(gdn["d"], 14 * s + 12 + d + 1)
                    pe.wait_ge(gdn["tok"], 2 * s + d + 1)
                    heads(2 + d, lambda hd: bM[:, d, hd, :], lambda hd: bT[:, d, hd, :], gdn["nw"])
                for d in range(2):
                    pe.wait_ge(gdn["nwc"], 2 * s + d + 1)
                    pe.wait_ge(gdn["S"], 2 * s + d + 1)
                    for hd in range(H1):
                        mm(bank(4 + d, H1, P)[:, hd, :], bT[:, d, hd, :], bD[:, d, hd, :], True, False)
                        mm(bank(4 + d, H1, P)[:, hd, :], bU[:, d, hd, :], bS[:, d, hd, :], False, True,
                           inc=gdn["vn"] if hd == H1 - 1 else None)
                for d in range(2):
                    pe.wait_ge(gdn["vnc"], 2 * s + d + 1)
                    if xs:
                        for hd in range(H1):
                            mm(bank(6 + d, H1, P)[:, hd, :], bS[:, d, hd, :], bQ[:, d, hd, :], True, False)
                            mm(bank(6 + d, H1, P)[:, hd, :], bV[:, d, hd, :], bA[:, d, hd, :], False, True)
                    heads(d, lambda hd: bC[:, d, hd, :], lambda hd: bV[:, d, hd, :], gdn["st"])

            pe.wait_ge(o_sq, 1)
            for k in range(2):
                mm(bank(2 + k, 512), ones, sqo[:, 2 * k:2 * k + 2, :].rearrange("p h t -> p (h t)"),
                   inc=o_ps if k else None)

            pe.wait_ge(o_ok, 1)
            for k in range(S_OUT):
                s = arrive()
                for half in range(2):
                    b = job_bank()
                    for c in range(KC):
                        mm(bank(b, T), wA(s, c, half), catF[:, c, :] if c < 4 else oT[:, c - 4, :], c == 0, c == KC - 1,
                           proj_ps if c == KC - 1 else None)
                release()

            sum_squares([(sq, range(KC))], T)
            pe.wait_ge(h_ok, norms[0])
            rw = PR("wroute", KC, 36)
            b = job_bank()
            for t in range(TT):
                for c in range(KC):
                    mm(bank(b, TT, 36)[:, t, :], h2[:, c, t * P:t * P + P], rw[:, c, :], c == 0, c == KC - 1,
                       proj_ps if c == KC - 1 and t == 1 else None)
            for g in range(NEXP // 2):
                pe.wait_ge(dg_ok, g + 1)
                if g >= 2:
                    pe.wait_ge(wr_ok, g - 1)
                mm(bank(g % 2, 512), ones, diag[:, g % 2 * 2:g % 2 * 2 + 2, :].rearrange("p e t -> p (e t)"), inc=wr_ps)

            zero_l, zero_r = arena[:, 12800:12928], arena[:, 12928:13440]
            pe.wait_ge(hid_ok, 2)
            for b in range(4):
                mm(bank(4 + b, 512), zero_l, zero_r, True, False, skip=True)
            p0 = pos[0]
            assert p0 == S_PRE and not pend[0]
            with pe.Fori(0, NEXP // 2) as i:
                for u in range(2):
                    for j in range(2):
                        pe.wait_ge(hid_ok, i * 4 + (2 * u + j + 1))
                        for w in range(2):
                            n = p0 + 6 * u + 2 * j + w
                            pe.wait_ge(full[n % SLOTS], i * 16 + 16 * (n // SLOTS + 1))
                            for half in range(2):
                                for c in range(KC):
                                    last = c == KC - 1
                                    mm(bank(2 * j + w, 2, T)[:, half, :], wA(n, c, half), h2[:, c, :], c == 0, last,
                                       gu_ps if last and half and w else None)
                            if w == 0:
                                release()
                        release()
                    for kk in range(2):
                        pe.wait_ge(hid_ok, i * 4 + (2 * u + kk + 3))
                        for o in range(KC):
                            n = p0 + 6 * u + 4 + o // 4
                            if kk == 0 and o % 4 == 0:
                                pe.wait_ge(full[n % SLOTS], i * 16 + 16 * (n // SLOTS + 1))
                            for k in (2 * kk, 2 * kk + 1):
                                ins = nc.tensor.matmul(
                                    bank(4 + o // 2, 2, T)[:, o % 2, :],
                                    ring[:, n % SLOTS, k * 512 + o % 4 * P:k * 512 + o % 4 * P + P], hid[:, k, :],
                                    start=False, stop=False, skip_group_check=True)
                                if pend[0]:
                                    ins.then_inc(free, pend[0])
                                    pend[0] = 0
                            if kk == 1 and o % 4 == 3:
                                ins.then_inc(free, 1)
            pos[0] = p0 + S_MOE
            mm(bank(0, 1), ident, ident[:, 0:1], inc=moe_ps)
            sum_squares([(sq, range(KC))], T)

            pe.wait_ge(mem_sq, 1)
            for c in range(KC):
                mm(bank(5, T), ones, cat[:, c, :], c == 0, c == KC - 1, inc=moe_ps if c == KC - 1 else None)

            for l in range(LAYERS):
                sum_squares([(sq, range(KC))], T)
                pe.wait_ge(h_ok, norms[0])
                h_ready = [norms[0]]
                for k in range(8):
                    s = arrive()
                    if k < 3:
                        for half in range(2 if k < 2 else 1):
                            job_a(s, half, h, T)
                        if k == 2:
                            job_b(s, h, 0, P, 32, tiles=2)
                    else:
                        job_b(s, h, 0, 0, T, tiles=2)
                    release()
                sum_squares([(sq, range(3)), (sq, range(3, 5))], T)
                pe.wait_ge(h_ok, norms[0])
                for k in range(2):
                    s = arrive()
                    for t in range(TT):
                        job_b(s, cv, t * P, 0, 384, kc=3, width=384)
                    release()
                s = arrive()
                for t in range(TT):
                    for n in range(2):
                        job_b(s, cv[:, 3:5, :], t * P, n * 512, 512, kc=2, width=1024)
                release()
                tq0 = 10 * l
                for k in range(10):
                    if k >= 4:
                        pe.wait_ge(tq_ev, tq0 + k - 3)
                    if k == 0:
                        pe.wait_ge(qk_ok, 3 * l + 1)
                    if k == 4:
                        pe.wait_ge(qk_ok, 3 * l + 2)
                    if k == 8:
                        pe.wait_ge(qk_ok, 3 * l + 3)
                    if k < 8:
                        src = qt if k < 4 else kc
                        for hh in range(2):
                            hd = 2 * (k % 4) + hh
                            for t in range(TT):
                                mm(bank(4 + k % 4, 2, T)[0:MLA_D, hh, t * P:t * P + P],
                                   src[:, t, hd * MLA_D:hd * MLA_D + MLA_D], ident, tr=True,
                                   inc=tq_ps if hh and t else None)
                    else:
                        for c in range(2):
                            for t in range(TT):
                                mm(bank(4 + k % 4, 2, T)[:, c, t * P:t * P + P],
                                   dt_[:, t, (k - 8) * 256 + c * P:(k - 8) * 256 + c * P + P], ident, tr=True,
                                   inc=tq_ps if c and t else None)
                pe.wait_ge(tq_ev, tq0 + 10)

                def scores(g, q, u):
                    if g >= 2:
                        pe.wait_ge(exp_ok, g - 1)
                    for c in range(2 if 8 <= u < 12 else 1):
                        for t in range(TT):
                            o = bank(2 * q + c, TT, T)[:, t, :]
                            last = t == 1 and (c == 1 or not 8 <= u < 12)
                            if u < 8:
                                mm(o, QT[0:MLA_D, u, t * P:t * P + P], KT[0:MLA_D, u, :], inc=sc_ps if last else None)
                            elif u < 12:
                                r = 64 * (u % 2) + 32 * c
                                mm(o, dqT[r:r + 32, (u - 8) // 2, t * P:t * P + P], dkT[r:r + 32, (u - 8) // 2, :],
                                   inc=sc_ps if last else None)
                            else:
                                for dc in range(2):
                                    mm(o, qm[:, 2 * (u - 12) + dc, t * P:t * P + P], km[:, 2 * (u - 12) + dc, :],
                                       dc == 0, dc == 1, inc=sc_ps if last and dc else None)

                def values(g, q, u):
                    pe.wait_ge(p_ok, g + 1)
                    if g >= 2:
                        pe.wait_ge(pt_ev, g - 1)
                    for kt in range(TT):
                        for t in range(TT):
                            mm(bank(4 + q, TT, T)[:, kt, t * P:t * P + P], Pb[q][:, t, kt * P:kt * P + P], ident,
                               tr=True, inc=pt_ps if kt and t else None)
                    pe.wait_ge(pt_ev, g + 1)
                    if g >= 2:
                        pe.wait_ge(o2_ev, g - 1)
                    for k in range(1 if u < 8 else 2):
                        for kt in range(TT):
                            if u < 8:
                                r = 64 * (u % 2)
                                mm(bank(6 + q, T)[r:r + 64, :], vt[:, kt, u * 64:u * 64 + 64], PTb[q][:, kt, :],
                                   kt == 0, kt == 1, inc=o2_ps if kt else None)
                            elif u < 12:
                                mm(bank(6 + q, TT, 64)[:, k, :], PTb[q][:, kt, k * P:k * P + P],
                                   dt_[:, kt, 512 + (u - 8) * 64:512 + (u - 8) * 64 + 64],
                                   kt == 0, kt == 1, inc=o2_ps if kt and k else None)
                            else:
                                mm(bank(6 + q, TT, T)[:, k, :],
                                   vm[:, kt, (u - 12) * 256 + k * P:(u - 12) * 256 + k * P + P], PTb[q][:, kt, :],
                                   kt == 0, kt == 1, inc=o2_ps if kt and k else None)

                def attention(units):
                    scores(16 * l + units[0], units[0] % 2, units[0])
                    for u in units:
                        if u + 1 in units:
                            scores(16 * l + u + 1, (u + 1) % 2, u + 1)
                        values(16 * l + u, u % 2, u)

                attention(range(12))
                pe.wait_ge(o2_ev, 16 * l + 12)
                pe.wait_ge(ld_sgu, 16 * (l + 1))
                for t in range(TT):
                    for g in range(4):
                        mm(bank(4, TT * 4, 64)[:, 4 * t + g, :], sguw[:, g, :], zt[:, t, 256 + 64 * g:256 + 64 * g + 64],
                           inc=mix_ps if t and g == 3 else None)
                for k in range(2):
                    pe.wait_ge(ot_ok, 2 * l + k + 1)
                    src = ob if k == 0 else ot
                    for c in range(2):
                        for t in range(TT):
                            mm(bank(6 + k, 2, T)[:, c, t * P:t * P + P], src[:, t, c * P:c * P + P], ident, tr=True,
                               inc=tc_ps if c and t else None)
                pe.wait_ge(cat_ok, 2 * l + 2)
                for k in range(4):
                    s = arrive()
                    for half in range(2):
                        job_a(s, half, cat, T)
                    release()
                sum_squares([(sq, range(KC))], T)
                sum_squares([(sq, range(KC))], T)
                pe.wait_ge(h_ok, norms[0])
                for k in range(12):
                    if k == 4:
                        pe.wait_ge(memn_ok, l + 1)
                    s = arrive()
                    if k < 8:
                        for half in range(2):
                            job_a(s, half, h if k < 4 else memn, T)
                    else:
                        job_b(s, memn, 0, 0, T, tiles=2)
                    release()
                pe.wait_ge(proj_ev, jobs[0])
                attention(range(12, 16))
                pe.wait_ge(o2_ev, 16 * l + 16)
                for k in range(4):
                    s = arrive()
                    for half in range(2):
                        job_a(s, half, cat, T)
                    release()
                sum_squares([(sq, range(KC))], T)
                sum_squares([(sq, range(KC))], T)
                pe.wait_ge(h_ok, norms[0])

                def up(i):
                    f = FFN_PAIRS * l + i
                    if f >= 2:
                        pe.wait_ge(f_ok, f - 1)
                    for w in range(2):
                        s = arrive()
                        for half in range(2):
                            for c in range(KC):
                                last = c == KC - 1
                                mm(bank(2 * (f % 2) + w, 2, T)[:, half, :], wA(s, c, half), h[:, c, :], c == 0, last,
                                   up_ps if last and half and w else None)
                        release()

                def down(i):
                    f = FFN_PAIRS * l + i
                    s = arrive()
                    pe.wait_ge(f_ok, f + 1)
                    for o in range(KC):
                        for k in range(2):
                            mm(bank(4 + o // 2, 2, T)[:, o % 2, :],
                               ring[:, s % SLOTS, k * 1024 + o * P:k * 1024 + o * P + P], fT[:, f % 2, k, :],
                               i == 0 and k == 0 and o % 2 == 0, False, skip=True,
                               inc=ffn_ps if i == FFN_PAIRS - 1 and k and o == KC - 1 else None)
                    release()

                up(0)
                for i in range(FFN_PAIRS):
                    if i + 1 < FFN_PAIRS:
                        up(i + 1)
                    down(i)
                pe.wait_ge(y_ok, l + 1)
                sum_squares([(sq, range(KC))], T)

        @block.scalar
        def _(act):
            act.dma_start(par[:, :], par_d).then_inc(ld_par, 16)
            act.dma_start(cst[:, :], cst_d).then_inc(ld_par, 16)
            act.dma_start(row[:, :], row_d).then_inc(ld_par, 16)
            act.dma_start(ctxT, xc_d[0]).then_inc(ld_x, 16)
            act.dma_start(xT[:, :, :], xc_d[1]).then_inc(ld_x, 16)
            act.dma_start(ipos[:, :], pos_d).then_inc(ld_x, 16)
            A_ = nc.scalar.activation
            signal = new_signal(act)
            jobs, norms = [0], [0]

            def take():
                act.wait_ge(proj_ps, jobs[0] + 1)
                jobs[0] += 1
                return (jobs[0] - 1) % 4

            def evac(dst, src, fn=ACT.Copy, done=True):
                i = A_(dst, src, fn)
                if done:
                    i.then_inc(proj_ev, 1)

            def squares(dst, src, after=None):
                norms[0] += 1
                if after is not None:
                    act.wait_ge(h_ok, after)
                A_(dst, src, ACT.Square).then_inc(sq_ok, 1)

            def root(dst, src, n):
                return A_(dst, src, ACT.Sqrt, scale=1.0 / n, bias=EPS)

            def norm_root(dst=rs[:, 0:T]):
                act.wait_ge(ss_ps, norms[0])
                root(dst, bank(4, T), D).then_inc(root_ok, 1)

            act.wait_ge(ld_par, 48)
            act.wait_ge(ld_x, 48)
            A_(sqA[:, :, 0:T], ctxT, ACT.Square)
            squares(sqA[:, :, T:2 * T], xT[:, :, :])
            A_(silu_c, PR("c", KC, 2), ACT.Silu).then_inc(silu_c_ok, 1)
            act.wait_ge(ss_ps, 1)
            root(rsA, bank(4, 2 * T), D).then_inc(root_ok, 1)
            act.wait_ge(rope_v, 1)
            A_(sinx, angk, ACT.Sin)
            A_(cosx, ang, ACT.Sin).then_inc(rope_a, 1)
            act.wait_ge(rope_v, 2)
            A_(lam_s, lam_s, ACT.Exp)
            A_(nega, RW("alog"), ACT.Exp).then_inc(rope_a, 1)

            b = take()
            evac(graw.rearrange("p t k -> p (t k)"), bank(b, 64))
            act.wait_ge(proj_ev, 1)
            A_(beta.rearrange("p d t h -> p t d h"), graw[:, :, 0:8].rearrange("p t (d h) -> p t d h", d=2),
               ACT.Sigmoid).then_inc(gate_a, 1)
            act.wait_ge(gate_v, 1)
            signal(A_(gtmp2, gtmp2, ACT.Exp, scale=-1.0), a_step)
            A_(gtmp2, gtmp2, ACT.Ln, bias=1.0).then_inc(gate_a, 1)

            for k in range(2):
                for t in range(TT):
                    b = take()
                    evac(ft[:, t, k * T:k * T + T], bank(b, T))
            act.wait_ge(zeroed, 1)

            def smooth(j):
                act.wait_ge(conv_ok, j + 1)
                v = qT[:, j, :] if j < 4 else kT[:, j - 4, :] if j < 8 else vT[:, j - 8, :]
                A_(v, v, ACT.Silu).then_inc(act_ok, 1)

            for j in range(16):
                b = take()
                if j < 12:
                    grid = padx[:, j, :].rearrange("p (r c) -> p r c", c=PW)[:, 1:1 + GRID_R, 1:1 + GRID_W]
                    src = bank(b, T) if j < 4 else bank(b, 2 * T)
                    if j >= 4:
                        evac(padc[:, j - 4, 1:1 + T], src[:, 0:T], done=False)
                        src = src[:, T:2 * T]
                    evac(grid, src.rearrange("p (r c) -> p r c", c=GRID_W))
                else:
                    evac(zT[:, j - 12, :], bank(b, T), ACT.Silu)
                if 2 <= j < 14:
                    smooth(j - 2)
            act.wait_ge(proj_ps, jobs[0])
            act.dma_start(dftT, dft_d).then_inc(ld_dft, 16)
            act.wait_ge(act_ok, 12)
            A_(sqk, kT, ACT.Square).then_inc(l2_sq, 1)
            A_(sqq, qT, ACT.Square).then_inc(l2_sq, 1)
            act.wait_ge(l2_ps, 1)
            root(rsk.rearrange("p h t -> p (h t)"), bank(0, 8 * T), 1).then_inc(root_ok, 1)
            root(rsq.rearrange("p h t -> p (h t)"), bank(4, 4 * T), 1).then_inc(root_ok, 1)
            act.wait_ge(gate_v, 3)
            A_(eg, gc, ACT.Exp)
            A_(ed, ed, ACT.Exp)
            A_(et, et, ACT.Exp).then_inc(gate_a, 1)
            for g in range(4):
                act.wait_ge(four_ps, 2 * g + 1)
                A_(dftG[:, g % 2, :], bank(g % 2, 2 * T), ACT.Copy).then_inc(four_g, 1)
                act.wait_ge(four_ps, 2 * g + 2)
                A_(catF[:, g, :], bank(2 + g % 2, T), ACT.Copy).then_inc(four_cat, 1)
            for s in range(4):
                for d in range(2):
                    act.wait_ge(gdn["pre"], 2 * s + d + 1)
                    A_(bC[:, d], bC[:, d], ACT.Exp).then_inc(gdn["exp"], 1)
                    if s >= 2:
                        A_(bQ[:, d], bank(d, H1, P), ACT.Exp).then_inc(gdn["eq"], 1)
                for v in range(1, len(LEVELS)):
                    for d in range(2):
                        act.wait_ge(gdn["u"], 14 * s + 2 * v + d + 1)
                        A_(bU[:, d], bank(d, H1, P), ACT.Copy).then_inc(gdn["uc"], 1)
                for d in range(2):
                    act.wait_ge(gdn["nw"], 2 * s + d + 1)
                    A_(bU[:, d], bank(2 + d, H1, P), ACT.Copy, scale=-1.0).then_inc(gdn["nwc"], 1)
                for d in range(2):
                    act.wait_ge(gdn["vn"], 2 * s + d + 1)
                    A_(bV[:, d], bank(4 + d, H1, P), ACT.Copy).then_inc(gdn["vnc"], 1)
            act.wait_ge(gdn["S"], 10)
            A_(sqo, oT, ACT.Square).then_inc(o_sq, 1)
            act.wait_ge(o_ps, 1)
            root(rso.rearrange("p h t -> p (h t)"), bank(2, 4 * T), P).then_inc(root_ok, 1)
            for j in range(8):
                b = take()
                evac(yb[:, j, :], bank(b, T))
            act.wait_ge(x_ok, 1)
            squares(sq, xT[:, :, :])
            norm_root()
            b = take()
            evac(logits, bank(b, TT, 36))
            act.wait_ge(rt_v, 1)
            A_(r4a, r4a, ACT.Exp)
            A_(r1v[:, 2], r1v[:, 2], ACT.Exp).then_inc(rt_a, 1)
            for g in range(NEXP // 2):
                act.wait_ge(wr_ps, g + 1)
                A_(wrow[:, 2 * g:2 * g + 2, :], bank(g % 2, 2, T), ACT.Copy).then_inc(wr_ok, 1)
            with act.Fori(0, NEXP // 2) as i:
                for u in range(2):
                    for j in range(2):
                        act.wait_ge(gu_ps, i * 4 + (2 * u + j + 1))
                        A_(sg[:, j], bank(2 * j, 2, T), ACT.Silu).then_inc(sg_ok, 1)
            act.wait_ge(moe_ps, 1)
            act.dma_start(memN, mem_d).then_inc(ld_mem, 16)
            act.wait_ge(x_ok, 2)
            squares(sq, xT[:, :, :])
            norm_root()
            act.wait_ge(ld_mem, 16)
            A_(cat, memN, ACT.Square).then_inc(mem_sq, 1)
            act.wait_ge(moe_ps, 2)
            root(rs[:, T:2 * T], bank(5, T), D).then_inc(root_ok, 1)

            for l in range(LAYERS):
                n0 = 3 + 7 * l
                g0 = 16 * l
                squares(sq, xT[:, :, :], n0)
                if l == 0:
                    act.wait_ge(mem_ok, 1)
                norm_root()
                for j in range(5):
                    b = take()
                    evac(cv[:, j, :], bank(b, T))
                b = take()
                evac(krt, bank(b, TT, 32))
                act.wait_ge(proj_ev, jobs[0] - 1)
                squares(sq[:, 0:5, :], cv)
                for k in range(5):
                    b = take()
                    if k < 2:
                        evac(zt[:, :, k * T:k * T + T], bank(b, TT, T), ACT.Gelu_apprx_tanh)
                    else:
                        evac(dt_[:, :, (k - 2) * T:(k - 1) * T], bank(b, TT, T))
                act.wait_ge(ss_ps, norms[0])
                root(rs[:, 0:T], bank(4, T), 384)
                root(rs[:, T:2 * T], bank(4, 2 * T)[:, T:2 * T], 256).then_inc(root_ok, 1)
                act.wait_ge(ln_ok, 2 * l + 1)
                root(st8b, st8b, 64).then_inc(root_ok, 1)
                for k in range(2):
                    for t in range(TT):
                        b = take()
                        evac(qt[:, t, k * 384:k * 384 + 384], bank(b, 384))
                for t in range(TT):
                    for n in range(2):
                        b = take()
                        src = bank(b, 4, P)
                        evac(kc[:, t, n * 384:n * 384 + 384].rearrange("p (h d) -> p h d", h=4)[:, :, 0:64],
                             src[:, :, 0:64], done=False)
                        evac(vt[:, t, n * 256:n * 256 + 256].rearrange("p (h d) -> p h d", h=4), src[:, :, 64:128])
                for k in range(10):
                    act.wait_ge(tq_ps, 10 * l + k + 1)
                    src = bank(4 + k % 4, 2, T)
                    if k < 8:
                        dst = (QT if k < 4 else KT)[0:MLA_D, 2 * (k % 4):2 * (k % 4) + 2, :]
                        A_(dst, src[0:MLA_D], ACT.Copy).then_inc(tq_ev, 1)
                    else:
                        A_(dqT if k == 8 else dkT, src, ACT.Copy).then_inc(tq_ev, 1)
                act.dma_start(sguw, sguw_d[l]).then_inc(ld_sgu, 16)

                def exps(u):
                    g, q = g0 + u, u % 2
                    act.wait_ge(max_ok, g + 1)
                    scale = (MLA_D if u < 8 else 32 if u < 12 else 256) ** -0.5
                    n = 4 if 8 <= u < 12 else 2
                    for k in range(n):
                        i = A_(Pb[2 * (k // 2) + q][:, k % 2, :], bank(2 * q + k // 2, TT, T)[:, k % 2, :], ACT.Exp,
                               bias=nmx[:, q, k:k + 1], scale=scale, accum_out=rsum[:, q, k:k + 1])
                    i.then_inc(exp_ok, 1)

                def outs(u):
                    g, q = g0 + u, u % 2
                    act.wait_ge(pt_ps, g + 1)
                    A_(PTb[q], bank(4 + q, TT, T), ACT.Copy).then_inc(pt_ev, 1)
                    act.wait_ge(o2_ps, g + 1)
                    if u < 8:
                        r = 64 * (u % 2)
                        A_(cat[r:r + 64, u // 2, :], bank(6 + q, T)[r:r + 64, :], ACT.Copy).then_inc(o2_ev, 1)
                    elif u < 12:
                        A_(ot[:, :, (u - 8) * 64:(u - 8) * 64 + 64], bank(6 + q, TT, 64), ACT.Copy).then_inc(o2_ev, 1)
                    else:
                        A_(cat[:, 2 * (u - 12):2 * (u - 12) + 2, :], bank(6 + q, TT, T), ACT.Copy).then_inc(o2_ev, 1)

                def attention(units):
                    exps(units[0])
                    for u in units:
                        if u + 1 in units:
                            exps(u + 1)
                        outs(u)

                attention(range(12))
                act.wait_ge(ln_ok, 2 * l + 2)
                root(st8, st8, 64).then_inc(root_ok, 1)
                for k in range(2):
                    act.wait_ge(tc_ps, 2 * l + k + 1)
                    A_(cat[:, 4 + 2 * k:6 + 2 * k, :], bank(6 + k, 2, T), ACT.Copy).then_inc(cat_ok, 1)
                for j in range(8):
                    b = take()
                    evac(yb[:, j, :], bank(b, T))
                act.wait_ge(proj_ev, jobs[0])
                squares(sq, yb)
                norm_root()
                squares(sq, xT[:, :, :], n0 + 3)
                norm_root()
                for j in range(8):
                    b = take()
                    evac(qm[:, j, :], bank(b, T))
                for j in range(8):
                    b = take()
                    evac(km[:, j, :], bank(b, T))
                for j in range(4):
                    b = take()
                    evac(vm[:, :, j * T:j * T + T], bank(b, TT, T))
                attention(range(12, 16))
                for j in range(8):
                    b = take()
                    evac(yb[:, j, :], bank(b, T))
                act.wait_ge(proj_ev, jobs[0])
                squares(sq, yb)
                norm_root()
                squares(sq, xT[:, :, :], n0 + 5)
                norm_root()
                for i in range(FFN_PAIRS):
                    f = FFN_PAIRS * l + i
                    q = f % 2
                    act.wait_ge(up_ps, f + 1)
                    for k in range(4):
                        ch = 2 * i + k % 2 + 22 * (k // 2)
                        a = A_(ca[:, q, k, :], bank(2 * q + k // 2, 2, T)[:, k % 2, :], ACT.Identity,
                               bias=PR(f"fbias{l}")[:, ch:ch + 1], scale=PR(f"fconv{l}", 3, 44)[:, 1, ch:ch + 1])
                    a.then_inc(tap_ok, 1)
                    act.wait_ge(conv2_ok, f + 1)
                    A_(ca[:, q, 0:2, :], ca[:, q, 0:2, :], ACT.Gelu_apprx_tanh).then_inc(gelu_ok, 1)
                act.wait_ge(ffn_ps, l + 1)
                A_(yb, bank(4, KC, T), ACT.Copy).then_inc(y_ok, 1)
                act.wait_ge(y_ok, l + 1)
                squares(sq, yb)
                norm_root()
            act.wait_ge(h_ok, 3 + 7 * LAYERS)
            act.dma_start(out_d, xT[:, :, :]).then_inc(out_done, 16)
            act.wait_ge(out_done, 16)

        @block.vector
        def _(dve):
            V = nc.vector
            link = new_step(dve, v_step)
            signal = new_signal(dve)
            MUL, ADD, SUB, MAX = ALU.mult, ALU.add, ALU.subtract, ALU.max

            def tt(out, a, b, op=MUL):
                return V.tensor_tensor(out, a, b, op)

            def ts(out, a, s1, op0, s2=None, op1=None):
                return V.tensor_scalar(out, a, s1, s2, op0, op1) if op1 is not None else V.tensor_scalar(out, a, s1, None, op0)

            def stt(out, a, s1, b, op0=MUL, op1=ADD):
                return V.scalar_tensor_tensor(out, a, s1, b, op0, op1)

            roots = [0]

            def rstd(v):
                roots[0] += 1
                dve.wait_ge(root_ok, roots[0])
                link(V.reciprocal(v, v))

            dve.wait_ge(ld_par, 48)
            dve.wait_ge(ld_x, 48)
            link(V.tensor_copy(posf, ipos[:, :]))
            link(tt(ang, over(posf, [P, TT, N_FREQ], 2), over(C("invf"), [P, TT, N_FREQ])))
            magic = 1.5 * 2.0 ** 23
            link(ts(angk, ang, 0.15915494309189535, MUL, magic, ADD))
            link(ts(angk, angk, magic, SUB))
            for part in (6.28125, 0.0019350051879882812, 3.0199158e-07):
                link(stt(ang, angk, -part, ang))
            pi = 3.1415925
            link(ts(angk, ang, pi, ALU.min, -pi, MAX))
            link(ts(ang, ang, 1.5707963267948966, ADD))
            link(ts(cosx, ang, pi, ALU.is_gt, -6.283185307179586, MUL))
            link(tt(ang, ang, cosx, ADD))
            signal(ts(ang, ang, pi, ALU.min, -pi, MAX), rope_v)
            for l in range(LAYERS):
                v = RW(f"lam{l}", 2, 2, 32)
                link(tt(lam_p, v[:, :, 0, :], v[:, :, 1, :]))
                link(V.tensor_reduce(lam_s[:, 2 * l:2 * l + 2], lam_p, axis=AX.X, op=ADD))
            signal(ts(nmx[:, 0, :], lam_s, 0.0, ADD), rope_v)
            dve.wait_ge(rope_a, 2)
            for l in range(LAYERS):
                init = 0.8 - 0.6 * 2.718281828459045 ** (-0.3 * l)
                link(tt(nlam[:, l:l + 1], lam_s[:, 2 * l + 1:2 * l + 2], lam_s[:, 2 * l:2 * l + 1], SUB))
                link(ts(nlam[:, l:l + 1], nlam[:, l:l + 1], -init, ADD))

            norms = [0]
            rstd(rsA)
            link(tt(sqA[:, :, 0:T], ctxT, over(rsA[:, 0:T], [P, KC, T])))
            link(tt(sqA[:, :, T:2 * T], xT[:, :, :], over(rsA[:, T:2 * T], [P, KC, T])))
            dve.wait_ge(mod_ps, 1)
            link(tt(mods, bank(5, 6 * KC, 2), over(PR("bmod"), [P, 6 * KC, 2], 2), ADD))
            link(stt(mulx, mods[:, KC:2 * KC, 0], 1.0, PR("norm1"), ADD, MUL))
            link(stt(mulc, mods[:, KC:2 * KC, 1], 1.0, PR("norm1"), ADD, MUL))
            link(stt(mul2, mods[:, 4 * KC:5 * KC, 0], 1.0, PR("norm2"), ADD, MUL))
            for c in range(KC):
                ts(hA[:, c, 0:T], sqA[:, c, 0:T], mulc[:, c:c + 1], MUL, mods[:, c, 1:2], ADD)
                i = ts(hA[:, c, T:2 * T], sqA[:, c, T:2 * T], mulx[:, c:c + 1], MUL, mods[:, c, 0:1], ADD)
            signal(i, h_ok)

            dve.wait_ge(proj_ev, 1)
            link(tt(gtmp, graw[:, :, 8:16], over(RW("dtb"), [P, 4, 8]), ADD))
            signal(stt(gtmp2, gtmp, -1.0, gtmp, MUL, MAX), gate_v)
            dve.wait_ge(gate_a, 2)
            link(stt(gtmp, gtmp, 0.0, gtmp2, MAX, ADD))
            link(ts(gtmp, gtmp, -1.0, MUL))
            signal(tt(gt.rearrange("p d t h -> p t d h"), gtmp.rearrange("p t (d h) -> p t d h", d=2),
                      nega.rearrange("p (d h) -> p d h", d=2).unsqueeze(1).to_broadcast([P, 4, 2, H1])), gate_v)

            cw = PR("conv", 9, 12)
            dve.wait_ge(zeroed, 1)
            for j in range(12):
                dve.wait_ge(proj_ev, 5 + j + 1)
                g = padx[:, j, :].rearrange("p (r c) -> p r c", c=PW)
                dst = qT[:, j, :] if j < 4 else (kT[:, j - 4, :] if j < 8 else vT[:, j - 8, :])
                dx = (dst if j < 4 else dst[:, T:2 * T]).rearrange("p (r c) -> p r c", c=GRID_W)
                taps = [4, 0, 1, 2, 3, 5, 6, 7, 8]
                for n, k in enumerate(taps):
                    src = g[:, k // 3:k // 3 + GRID_R, k % 3:k % 3 + GRID_W]
                    w = cw[:, k, j:j + 1]
                    ins = [ts(dx, src, w, MUL) if n == 0 else stt(dx, src, w, dx)]
                    if j >= 4 and n < 3:
                        k1 = [4, 3, 5][n]
                        src = padc[:, j - 4, k1 - 3:k1 - 3 + T]
                        w = cw[:, k1, j:j + 1]
                        ins.append(ts(dst[:, 0:T], src, w, MUL) if n == 0 else stt(dst[:, 0:T], src, w, dst[:, 0:T]))
                    if n < 8:
                        link(ins[-1])
                    else:
                        ins[-1].then_inc(conv_ok, 1)

            rstd(rsk)
            rstd(rsq)
            link(stt(qT, qT, float(P) ** -0.5, rsq, MUL, MUL))
            signal(tt(kT, kT, rsk), l2_ok)
            dve.wait_ge(gate_ps, 1)
            link(V.tensor_copy(gc.rearrange("p d t h -> p (d t h)"), bank(6, 64)[:, 0:32]))
            link(V.tensor_copy(et.rearrange("p d t h -> p (d t h)"), bank(6, 64)[:, 32:64]))
            signal(tt(ed, et, gc, SUB), gate_v)
            dve.wait_ge(gate_a, 3)
            link(tt(beg, beta, eg))
            for d in range(2):
                signal(V.memset(bS[:, d], 0.0), gdn["S"])

            for s in range(4):
                tiles = (s, s ^ 1)
                xs = s >= 2
                full_h = [P, H1, P]

                def per_head(v, d):
                    return over(v[:, d, tiles[d], :], full_h, 2)

                for d in range(2):
                    link(tt(bD[:, d], over(C(f"cum{d}"), full_h), per_head(gt, d)))
                    signal(tt(bU[:, d], over(ident, full_h), per_head(beta, d)), gdn["rows"])
                for d in range(2):
                    dve.wait_ge(gdn["gb"], 2 * s + d + 1)
                    link(tt(bC[:, d], bank(d, H1, P), over(C(f"neg{d}"), full_h), ADD))
                    signal(tt(bC[:, d], bC[:, d], per_head(gc, d), SUB), gdn["pre"])
                for d in range(2):
                    dve.wait_ge(gdn["kk"], 2 * s + d + 1)
                    dve.wait_ge(gdn["exp"], 2 * s + d + 1)
                    link(tt(bM[:, d], bank(4 + d, H1, P), bC[:, d]))
                    if xs:
                        link(tt(bA[:, d], bank(6 + d, H1, P), bC[:, d]))
                        dve.wait_ge(gdn["eq"], 2 * (s - 2) + d + 1)
                        tq = (tiles[d] - 2) * P
                        link(tt(bQ[:, d], bQ[:, d], qT[:, :, tq:tq + P]))
                    link(tt(bM[:, d], bM[:, d], bank(2 + d, H1, P)))
                    signal(tt(bC[:, d], bM[:, d], over(C(f"lev{d}", 7, P)[:, 0, :], full_h)), gdn["ct"])
                for d in range(2):
                    link(tt(bT[:, d], bC[:, d], over(ident, full_h), ADD))
                    dve.wait_ge(gdn["u"], 14 * s + d + 1)
                    signal(tt(bD[:, d], bank(d, H1, P), over(ident, full_h), ADD), gdn["d"])
                for v in range(1, len(LEVELS)):
                    for d in range(2):
                        signal(tt(bC[:, d], bM[:, d], over(C(f"lev{d}", 7, P)[:, v, :], full_h)), gdn["ct"])
                    for d in range(2):
                        dve.wait_ge(gdn["vv"], 12 * s + 2 * (v - 1) + d + 1)
                        if v < len(LEVELS) - 1:
                            link(tt(bD[:, d], bD[:, d], bank(2 + d, H1, P), ADD))
                        signal(tt(bT[:, d], bT[:, d], bank(4 + d, H1, P), ADD), gdn["d"])
                for d in range(2):
                    dve.wait_ge(gdn["tr"], 2 * s + d + 1)
                    link(tt(bM[:, d], bank(d, H1, P), per_head(beg, d)))
                    link(tt(bC[:, d], bank(d, H1, P), per_head(ed, d)))
                    signal(tt(bD[:, d], bank(6 + d, H1, P), per_head(beta, d)), gdn["tok"])
                for d in range(2):
                    dve.wait_ge(gdn["st"], 2 * s + d + 1)
                    if xs:
                        tq = (tiles[d] - 2) * P
                        o = oT[:, :, tq:tq + P]
                        if s == 2:
                            link(V.tensor_copy(o, bank(6 + d, H1, P)))
                        else:
                            link(tt(o, o, bank(6 + d, H1, P), ADD))
                    link(tt(bS[:, d], bS[:, d], per_head(et, d)))
                    signal(tt(bS[:, d], bS[:, d], bank(d, H1, P), ADD), gdn["S"])

            rstd(rso)
            link(tt(oT, oT, rso))
            signal(stt(oT, oT, PR("onorm"), zT, MUL, MUL), o_ok)
            for c in range(KC):
                dve.wait_ge(proj_ev, 21 + c + 1)
                i = stt(xT[:, c, :], yb[:, c, :], mods[:, 2 * KC + c, 0:1], xT[:, c, :])
            signal(i, x_ok)

            def pre_norm(dst, g, b=None, src=xT, n=KC):
                rstd(rs[:, 0:T])
                link(tt(sq, src[:, :, :], over(rs[:, 0:T], [P, KC, T])))
                for c in range(KC):
                    i = ts(dst[:, c, :], sq[:, c, :], g[:, c:c + 1], MUL) if b is None else \
                        ts(dst[:, c, :], sq[:, c, :], g[:, c:c + 1], MUL, b(c), ADD)
                signal(i, h_ok)

            def post_norm(g):
                rstd(rs[:, 0:T])
                link(tt(yb, yb, over(rs[:, 0:T], [P, KC, T])))
                for c in range(KC):
                    i = stt(xT[:, c, :], yb[:, c, :], g[:, c:c + 1], xT[:, c, :])
                signal(i, h_ok)

            pre_norm(h2, mul2, lambda c: mods[:, 3 * KC + c, 0:1])

            dve.wait_ge(proj_ev, 30)
            m, den, m1, m2, w1, w2, dd = r1v[:, 0], r1v[:, 1], r1v[:, 3], r1v[:, 4], r1v[:, 5], r1v[:, 6], r1v[:, 2]
            lg, le = logits[:, :, 0:4], logits[:, :, 4:36]
            link(tt(lg, lg, over(RW("bgroup"), [P, TT, 4]), ADD))
            link(tt(le, le, over(RW("brouter"), [P, TT, 32]), ADD))

            def col(v, n):
                return over(v, [P, TT, n], 2)

            def first_max(onehot, mxv, src, tmp, first, n):
                link(V.tensor_reduce(mxv, src, axis=AX.X, op=MAX))
                link(tt(tmp, src, col(mxv, n), ALU.is_ge))
                link(tt(tmp, tmp, over(C(first), [P, TT, n])))
                link(V.tensor_reduce(den, tmp, axis=AX.X, op=MAX))
                link(tt(onehot, tmp, col(den, n), ALU.is_equal))

            first_max(r4b, m, lg, r4a, "first4", 4)
            link(tt(r4a, lg, col(m, 4), SUB))
            link(tt(elp.rearrange("p t (g e) -> p t g e", g=4), le.rearrange("p t (g e) -> p t g e", g=4),
                    r4b.unsqueeze(3).to_broadcast([P, TT, 4, 8])))
            link(V.tensor_reduce(r8a, elp.rearrange("p t (g e) -> p t e g", g=4), axis=AX.X, op=ADD))
            first_max(r8b, m1, r8a, r8c, "first8", 8)
            link(stt(r8a, r8b, NEG, r8a))
            first_max(r8c, m2, r8a, r8c, "first8", 8)
            signal(tt(dd, m2, m1, SUB), rt_v)
            dve.wait_ge(rt_a, 1)
            link(V.tensor_reduce(den, r4a, axis=AX.X, op=ADD))
            link(ts(w1, dd, 1.0, ADD))
            link(tt(w1, w1, den))
            link(V.reciprocal(w1, w1))
            link(tt(w2, w1, dd))
            link(tt(r8b, r8b, col(w1, 8)))
            link(tt(r8c, r8c, col(w2, 8)))
            link(tt(r8b, r8b, r8c, ADD))
            for t in range(TT):
                link(tt(comb[:, t, :].rearrange("p (g e) -> p g e", g=4), over(r4b[:, t, :], [P, 4, 8], 2),
                        over(r8b[:, t, :], [P, 4, 8])))
            for g in range(NEXP // 2):
                if g >= 2:
                    dve.wait_ge(wr_ps, g - 1)
                for e in range(2):
                    i = tt(diag[:, g % 2 * 2 + e, :].rearrange("p (t j) -> p t j", t=TT), over(ident, [P, TT, P]),
                           over(comb[:, :, 2 * g + e], [P, TT, P], 2))
                i.then_inc(dg_ok, 1)
            dve.wait_ge(wr_ok, NEXP // 2)
            V.memset(arena[:, 12800:12928], 0.0).then_inc(hid_ok, 1)
            V.memset(arena[:, 12928:13440], 0.0).then_inc(hid_ok, 1)
            with dve.Fori(0, NEXP // 2) as i:
                for u in range(2):
                    for j in range(2):
                        dve.wait_ge(sg_ok, i * 4 + (2 * u + j + 1))
                        tt(sg[:, j], sg[:, j], bank(2 * j + 1, 2, T)).then_inc(up_w, 1)
                        dve.wait_ge(up_w, i * 4 + (2 * u + j + 1))
                        tt(hid[:, 2 * j:2 * j + 2, :], sg[:, j],
                           over(arena[:, bass.ds(i * (2 * T) + (4608 + u * T), T)], [P, 2, T])).then_inc(hid_ok, 1)
            dve.wait_ge(moe_ps, 1)
            for c in range(KC):
                i = stt(xT[:, c, :], bank(4 + c // 2, 2, T)[:, c % 2, :], mods[:, 5 * KC + c, 0:1], xT[:, c, :])
            signal(i, x_ok)
            pre_norm(xT, PR("final"))
            rstd(rs[:, T:2 * T])
            signal(tt(memN, memN, over(rs[:, T:2 * T], [P, KC, T])), mem_ok)

            for l in range(LAYERS):
                n0 = 3 + 7 * l
                g0 = 16 * l
                e0 = 30 + 55 * l
                pre_norm(h, PR(f"mix_pre{l}"))
                rstd(rs)
                for c in range(5):
                    g = PR(f"cq{l}")[:, c:c + 1] if c < 3 else PR(f"ckv{l}")[:, c - 3:c - 2]
                    i = stt(cv[:, c, :], cv[:, c, :], g, rs[:, 0:T] if c < 3 else rs[:, T:2 * T], MUL, MUL)
                signal(i, h_ok)
                dve.wait_ge(proj_ev, e0 + 8)
                vv = zt[:, :, 256:512].rearrange("p t (g c) -> p t g c", g=4)
                s8 = [P, TT, 4, 64]
                st, stb = [x.rearrange("p (t g) -> p t g", t=TT) for x in (st8, st8b)]
                tmp = A(16704, TT, 4, 64)
                link(V.tensor_reduce(st, vv, axis=AX.X, op=ADD))
                link(ts(st8, st8, 1.0 / 64, MUL))
                link(tt(vv, vv, st.unsqueeze(3).to_broadcast(s8), SUB))
                link(tt(tmp, vv, vv))
                signal(V.tensor_reduce(stb, tmp, axis=AX.X, op=ADD), ln_ok)
                rstd(st8b)
                link(tt(vv, vv, stb.unsqueeze(3).to_broadcast(s8)))
                link(tt(zt[:, :, 256:512], zt[:, :, 256:512], over(RW(f"sgu_g{l}"), [P, TT, 256])))

                def rotate(x1, x2, c, s, o1, o2, t, put=None):
                    tt(t[0], x1, c)
                    tt(t[1], x2, s)
                    tt(t[2], x2, c)
                    link(tt(t[3], x1, s))
                    put = put or (lambda v: v)
                    tt(o1, put(t[0]), put(t[1]), SUB)
                    return tt(o2, put(t[2]), put(t[3]), ADD)

                def table(v, lo, n, k):
                    return v[:, :, lo:lo + n].unsqueeze(2).to_broadcast([P, TT, k, n])

                dve.wait_ge(proj_ev, e0 + 15)
                qv = qt.rearrange("p t (h d) -> p t h d", d=MLA_D)
                kv = kc.rearrange("p t (h d) -> p t h d", d=MLA_D)
                t8 = [rtmp[:, k].rearrange("p (t h d) -> p t h d", t=TT, h=8) for k in range(4)]
                i = rotate(qv[:, :, :, 64:80], qv[:, :, :, 80:96], table(cosx, 0, 16, 8), table(sinx, 0, 16, 8),
                           qv[:, :, :, 64:80], qv[:, :, :, 80:96], t8)
                signal(i, qk_ok)
                dve.wait_ge(proj_ev, e0 + 19)
                tk = [rtk[:, k].rearrange("p (t d) -> p t d", t=TT) for k in range(4)]
                i = rotate(krt[:, :, 0:16], krt[:, :, 16:32], cosx[:, :, 0:16], sinx[:, :, 0:16],
                           kv[:, :, :, 64:80], kv[:, :, :, 80:96], tk,
                           lambda v: v.unsqueeze(2).to_broadcast([P, TT, 8, 16]))
                signal(i, qk_ok)
                dv = dt_[:, :, 0:512].rearrange("p t (u d) -> p t u d", d=32)
                t16 = [rtmp[:, k].rearrange("p (t h d) -> p t h d", t=TT, h=16) for k in range(4)]
                i = rotate(dv[:, :, :, 0:8], dv[:, :, :, 8:16], table(cosx, 16, 8, 16), table(sinx, 16, 8, 16),
                           dv[:, :, :, 0:8], dv[:, :, :, 8:16], t16)
                signal(i, qk_ok)

                def maxima(u):
                    g, q = g0 + u, u % 2
                    dve.wait_ge(sc_ps, g + 1)
                    n = 4 if 8 <= u < 12 else 2
                    scale = (MLA_D if u < 8 else 32 if u < 12 else 256) ** -0.5
                    link(V.tensor_reduce(mx[:, q, 0:n], bank(2 * q, n, T), axis=AX.X, op=MAX))
                    signal(ts(nmx[:, q, 0:n], mx[:, q, 0:n], -scale, MUL), max_ok, False)

                def normalize(u):
                    g, q = g0 + u, u % 2
                    dve.wait_ge(exp_ok, g + 1)
                    n = 4 if 8 <= u < 12 else 2
                    link(V.reciprocal(rinv[:, q, 0:n], rsum[:, q, 0:n]))
                    if n == 2:
                        for t in range(TT):
                            i = ts(Pb[q][:, t, :], Pb[q][:, t, :], rinv[:, q, t:t + 1], MUL)
                    else:
                        link(ts(rinv[:, q, 2:4], rinv[:, q, 2:4], nlam[:, l:l + 1], MUL))
                        for t in range(TT):
                            i = ts(Pb[2 + q][:, t, :], Pb[2 + q][:, t, :], rinv[:, q, 2 + t:3 + t], MUL)
                        link(i)
                        for t in range(TT):
                            i = stt(Pb[q][:, t, :], Pb[q][:, t, :], rinv[:, q, t:t + 1], Pb[2 + q][:, t, :])
                    i.then_inc(p_ok, 1)

                def attention(units):
                    maxima(units[0])
                    for u in units:
                        if u + 1 in units:
                            maxima(u + 1)
                        normalize(u)

                attention(range(12))
                dve.wait_ge(mix_ps, l + 1)
                mixv = bank(4, TT * 4, 64)
                obv = ob.rearrange("p t (g c) -> p (t g) c", g=4)
                for t in range(TT):
                    i = tt(obv[:, 4 * t:4 * t + 4, :], mixv[:, 4 * t:4 * t + 4, :], over(PR(f"sgu_b{l}"), [P, 4, 64], 2), ADD)
                link(i)
                signal(tt(ob, ob, zt[:, :, 0:256]), ot_ok)
                dve.wait_ge(o2_ev, g0 + 12)
                otv = ot.rearrange("p t (h c) -> p t h c", h=4)
                link(tt(tmp, otv, otv))
                signal(V.tensor_reduce(st, tmp, axis=AX.X, op=ADD), ln_ok)
                rstd(st8)
                link(ts(st8, st8, 1.0 - (0.8 - 0.6 * 2.718281828459045 ** (-0.3 * l)), MUL))
                link(tt(otv, otv, st.unsqueeze(3).to_broadcast(s8)))
                signal(tt(ot.rearrange("p t (h c) -> p (t h) c", h=4), ot.rearrange("p t (h c) -> p (t h) c", h=4),
                          over(RW(f"sub_g{l}"), [P, TT * 4, 64])), ot_ok)
                post_norm(PR(f"mix_post{l}"))
                pre_norm(h, PR(f"mem_pre{l}"))
                g = PR(f"mem_kv{l}")
                for c in range(KC):
                    i = ts(memn[:, c, :], memN[:, c, :], g[:, c:c + 1], MUL)
                i.then_inc(memn_ok, 1)
                attention(range(12, 16))
                post_norm(PR(f"mem_post{l}"))
                pre_norm(h, PR(f"ffn_pre{l}"))
                fw = PR(f"fconv{l}", 3, 44)
                for i_ in range(FFN_PAIRS):
                    f = FFN_PAIRS * l + i_
                    q = f % 2
                    dve.wait_ge(tap_ok, f + 1)
                    for side in range(2):
                        for k in range(4):
                            ch = 2 * i_ + k % 2 + 22 * (k // 2)
                            src = bank(2 * q + k // 2, 2, T)[:, k % 2, :]
                            dst = ca[:, q, k, 1:T] if side == 0 else ca[:, q, k, 0:T - 1]
                            src = src[:, 0:T - 1] if side == 0 else src[:, 1:T]
                            i = stt(dst, src, fw[:, 2 * side, ch:ch + 1], dst)
                        if side == 0:
                            link(i)
                    signal(i, conv2_ok, False)
                    dve.wait_ge(gelu_ok, f + 1)
                    dve.wait_ge(conv2_ok, f + 1)
                    tt(fT[:, q], ca[:, q, 0:2, :], ca[:, q, 2:4, :]).then_inc(f_ok, 1)
                post_norm(PR(f"ffn_post{l}"))


def rows_of(v, k):
    return v.reshape(-1, k, 128).transpose(2, 0, 1).reshape(128, -1)


def tiles(w, n):
    k, m = w.shape
    return w.reshape(k // 128, 128, m // n, n).transpose(2, 1, 0, 3).reshape(m // n, 128, -1)


def kernel(**inputs):
    import numpy as np
    import concourse.bacc as bacc
    from concourse.bass_utils import run_bass_kernel_spmd

    a = {k: np.asarray(v) for k, v in inputs.items()}
    stream = np.zeros((S_ALL, P, SLOT), np.float32)
    at = [0]

    def put(t):
        stream[at[0]:at[0] + t.shape[0], :, :t.shape[2]] = t
        at[0] += t.shape[0]

    put(tiles(a["w_mod"][0], 256))
    w_in = a["w_in"][0]
    put(tiles(w_in[:, :2560], 256))
    put(tiles(a["w_out"][0], 256))
    for e in range(NEXP):
        g, u = tiles(a["w_gate"][0, e], 256), tiles(a["w_up"][0, e], 256)
        put(np.stack([g[0], u[0], g[1], u[1]]))
        put(tiles(a["w_down"][0, e], 512))
    for l in range(LAYERS):
        w = a["w_in_2"][l]
        wp = np.zeros((D, 2048), np.float32)
        wp[:, :672] = w[:, :672]
        wp[:, 768:] = w[:, 672:]
        put(tiles(wp, 256))
        put(tiles(a["mla_w_uq_2"][l], 384))
        put(tiles(a["mla_w_ukv_2"][l], 1024))
        put(tiles(a["w_mix_out_2"][l], 256))
        put(tiles(a["mem_w_q_2"][l], 256))
        put(tiles(a["mem_w_kv_2"][l], 256))
        put(tiles(a["mem_w_o_2"][l], 256))
        up, down = tiles(a["ffn_w_up_2"][l], 256), a["ffn_w_down_2"][l]
        down = down.reshape(FFN_PAIRS, 2, P, D).transpose(0, 2, 1, 3).reshape(FFN_PAIRS, P, 2 * D)
        for i in range(FFN_PAIRS):
            put(np.stack([up[i], up[FFN_PAIRS + i]]))
            if i:
                put(down[i - 1:i])
        put(down[FFN_PAIRS - 1:])
    assert at[0] == S_ALL

    par = np.zeros((P, N_PAR), np.float32)
    row = np.zeros((P, N_ROW), np.float32)

    def set_par(name, v):
        o, n = PAR[name]
        par[:, o:o + n] = v

    def set_row(name, v):
        o, n = ROW[name]
        row[:, o:o + n] = v.reshape(1, n)

    set_par("norm1", rows_of(a["norm1_g"], 8))
    set_par("norm2", rows_of(a["norm2_g"], 8))
    set_par("final", rows_of(a["final_g"], 8))
    set_par("bmod", rows_of(a["b_mod"], 48))
    set_par("c", np.stack([rows_of(a["c"], 8), rows_of(a["c_ctx"], 8)], 2).reshape(P, 16))
    set_par("conv", rows_of(a["conv_w"][0].reshape(9, 1536), 12))
    set_par("onorm", a["onorm_g"].reshape(P, 1))
    set_par("wgates", tiles(np.ascontiguousarray(w_in[:, 2560:]), 16)[0])
    set_par("wroute", tiles(np.concatenate([a["w_group"][0], a["w_router"][0]], 1), 36)[0])
    set_row("alog", a["a_log"])
    set_row("dtb", a["dt_bias"])
    set_row("bgroup", a["b_group"])
    set_row("brouter", a["b_router"])
    names = [("mix_pre", "mix_pre_g_2", 8), ("mix_post", "mix_post_g_2", 8), ("cq", "mla_cq_g_2", 3),
             ("ckv", "mla_ckv_g_2", 2), ("mem_pre", "mem_pre_g_2", 8), ("mem_post", "mem_post_g_2", 8),
             ("mem_kv", "mem_kv_g_2", 8), ("ffn_pre", "ffn_pre_g_2", 8), ("ffn_post", "ffn_post_g_2", 8),
             ("fconv", "ffn_conv_w_2", 44), ("fbias", "ffn_conv_b_2", 44)]
    for l in range(LAYERS):
        for name, key, k in names:
            set_par(f"{name}{l}", rows_of(a[key][l], k))
        set_par(f"sgu_b{l}", a["sgu_b_s_2"][l].T)
        set_row(f"sgu_g{l}", a["sgu_norm_g_2"][l])
        set_row(f"sub_g{l}", a["diff_sub_g_2"][l])
        set_row(f"lam{l}", np.concatenate([a[f"diff_lam_{n}_2"][l] for n in ("q1", "k1", "q2", "k2")]))

    def chan(v):
        return v.T.reshape(KC, P, T).transpose(1, 0, 2)

    cst, dft = constants()
    arrays = {
        "stream": stream, "par": par, "row": row, "cst": cst, "dft": dft,
        "xc": np.stack([chan(a["ctx"][0]), chan(a["x"][0])]),
        "mem": chan(a["mem_2"][0]),
        "pos": a["positions_2"].reshape(TT, P).T,
        "sguw": a["sgu_w_s_2"].transpose(0, 3, 1, 2),
    }
    nc = bacc.Bacc("TRN2", target_bir_lowering=False, num_devices=1)
    args = []
    arrays = {"in_" + k: np.ascontiguousarray(v) for k, v in arrays.items()}
    for k, v in arrays.items():
        args.append(nc.dram_tensor(k, v.shape, mybir.dt.from_np(v.dtype), kind="ExternalInput").ap())
    out = nc.dram_tensor("out_y", (P, KC, T), F32, kind="ExternalOutput").ap()
    trunk_kernel(nc, *args, out)
    r = run_bass_kernel_spmd(nc, [arrays], core_ids=[0])
    y = np.asarray(r.results[0]["out_y"])
    return np.ascontiguousarray(y.transpose(1, 0, 2).reshape(D, T).T).reshape(1, T, D)
```

```python
from contextlib import ExitStack

import concourse.bass as bass
from concourse import mybir

F32 = mybir.dt.float32
I32 = mybir.dt.int32
ALU = mybir.AluOpType
ACT = mybir.ActivationFunctionType
AX = mybir.AxisListType

P = 128
D = 1024
T = 256
TT = T // P
KC = D // P
EPS = 1e-6
H1 = 4
NEXP, NGRP, EPG = 32, 4, 8
DFF = 2816
GRID_R, GRID_W = 4, 64
PW = GRID_W + 2
SLOT = 2048
SLOTS = 12
NEG = -1.0e30
LEVELS = [1, 2, 4, 8, 16, 32, 64]
MLA_H, MLA_D, MLA_R = 8, 96, 32
DIFF_H = 4
XH = 4
N_FREQ = 24
LAYERS = 2
SLOTN = 64
PAIRS = NEXP // 2
FFN_PAIRS = DFF // 256

S_MOD, S_IN, S_OUT = 24, 10, 4
S_EXP = 6
S_PRE = S_MOD + S_IN + S_OUT
S_MOE = S_EXP * NEXP
S_LAYER = 8 + 2 + 1 + 4 + 4 + 8 + 4 + 3 * FFN_PAIRS
S_ALL = S_PRE + S_MOE + LAYERS * S_LAYER


def offsets(sizes):
    at, out = 0, {}
    for name, n in sizes:
        out[name] = (at, n)
        at += n
    return out, at


PAR_1 = [("norm1", KC), ("norm2", KC), ("final", KC), ("bmod", 6 * KC), ("c", 2 * KC), ("conv", 9 * 12),
         ("onorm", 1), ("wgates", KC * 16), ("wroute", KC * 36)]
PAR_L = [("mix_pre", KC), ("mix_post", KC), ("cq", 3), ("ckv", 2), ("mem_pre", KC), ("mem_post", KC),
         ("mem_kv", KC), ("ffn_pre", KC), ("ffn_post", KC), ("fconv", 3 * 44), ("fbias", 44), ("sgu_b", 4)]
PAR, N_PAR = offsets(PAR_1 + [(f"{n}{l}", k) for l in range(LAYERS) for n, k in PAR_L])
ROW_1 = [("alog", 8), ("dtb", 8), ("bgroup", 4), ("brouter", 32)]
ROW_L = [("sgu_g", 256), ("sub_g", 64), ("lam", 128)]
ROW, N_ROW = offsets(ROW_1 + [(f"{n}{l}", k) for l in range(LAYERS) for n, k in ROW_L])
CST, N_CST = offsets([("ident", P), ("ones", P), ("cum0", P), ("cum1", P), ("neg0", P), ("neg1", P),
                      ("lev0", P * len(LEVELS)), ("lev1", P * len(LEVELS)), ("dftc", 2 * P),
                      ("invf", N_FREQ), ("first4", 4), ("first8", 8), ("iota", SLOTN)])


def constants():
    import numpy as np
    c = np.zeros((P, N_CST), np.float32)

    def put(name, a):
        o, n = CST[name]
        c[:, o:o + n] = np.asarray(a, np.float64).reshape(P, n)

    i, j = np.arange(P)[None, :], np.arange(P)[:, None]
    put("ident", i == j)
    put("ones", np.ones((P, P)))
    put("cum0", j <= i)
    put("cum1", j >= i)
    put("neg0", np.where(j <= i, 0, NEG))
    put("neg1", np.where(j >= i, 0, NEG))
    lev = [-1.0 * ((j // (2 * s) == i // (2 * s)) & (j % (2 * s) < s) & (i % (2 * s) >= s)) for s in LEVELS]
    put("lev0", np.stack(lev, 1))
    put("lev1", np.stack([m.T for m in lev], 1))
    t = np.arange(T)
    ang = 2 * np.pi * ((t[:, None] * t[None, :]) % T) / T
    s = 1.0 / np.sqrt(T * P)
    dft = np.concatenate([np.cos(ang) * s, np.sin(ang) * s], 1).reshape(TT, P, 2 * T).transpose(1, 0, 2)
    t = np.arange(P)
    ang = 2 * np.pi * ((t[:, None] * t[None, :]) % P) / P
    put("dftc", np.concatenate([np.cos(ang), -np.sin(ang)], 1))
    f1 = np.float32(500000.0) ** (-np.arange(0, 32, 2, dtype=np.float32) / np.float32(32))
    f2 = np.float32(500000.0) ** (-np.arange(0, 16, 2, dtype=np.float32) / np.float32(16))
    put("invf", np.tile(np.concatenate([f1, f2]), (P, 1)))
    put("first4", np.tile(np.arange(4, 0, -1), (P, 1)))
    put("first8", np.tile(np.arange(8, 0, -1), (P, 1)))
    put("iota", np.tile(np.arange(SLOTN), (P, 1)))
    return c, np.ascontiguousarray(dft, np.float32)


def trunk_kernel(nc, stream, par_d, row_d, cst_d, dft_d, xc_d, mem_d, pos_d, sguw_d, out_d):
    ctx = ExitStack()
    with ctx:
        def sb(name, shape, dt=F32):
            return ctx.enter_context(nc.sbuf_tensor(name, shape, dt))

        def sem(name):
            return ctx.enter_context(nc.semaphore(name))

        ring = sb("ring", [P, SLOTS, SLOT])
        cst = sb("cst", [P, N_CST])
        par = sb("par", [P, N_PAR])
        row = sb("row", [P, N_ROW])
        xT = sb("xT", [P, KC, T])
        small = sb("small", [P, 1400])
        ipos = sb("ipos", [P, TT], I32)
        rounds_i = sb("rounds_i", [P, 1], I32)
        arena = sb("arena", [P, 19456])
        ps = ctx.enter_context(nc.psum_tensor("ps", [P, 8, 512], F32))

        def view(t, at, *dims):
            n = 1
            for d in dims:
                n *= d
            v = t[:, at:at + n]
            if len(dims) == 2:
                v = v.rearrange("p (a b) -> p a b", a=dims[0])
            elif len(dims) == 3:
                v = v.rearrange("p (a b c) -> p a b c", a=dims[0], b=dims[1])
            return v

        def C(name, *dims):
            o, n = CST[name]
            return view(cst, o, *(dims or (n,)))

        def PR(name, *dims):
            o, n = PAR[name]
            return view(par, o, *(dims or (n,)))

        def RW(name, *dims):
            o, n = ROW[name]
            return view(row, o, *(dims or (n,)))

        ident, ones = C("ident"), C("ones")
        sm_at = [0]

        def S(*dims):
            n = 1
            for d in dims:
                n *= d
            v = view(small, sm_at[0], *dims)
            sm_at[0] += n
            assert sm_at[0] <= 1400
            return v

        def bank(b, *dims):
            n = 1
            for d in dims:
                n *= d
            k = -(-n // 512)
            v = ps[:, b:b + k, :].rearrange("p a b -> p (a b)")[:, 0:n]
            if len(dims) == 2:
                v = v.rearrange("p (a b) -> p a b", a=dims[0])
            elif len(dims) == 3:
                v = v.rearrange("p (a b c) -> p a b c", a=dims[0], b=dims[1])
            return v

        def over(a, shape, axis=1):
            return a.unsqueeze(axis).to_broadcast(shape)

        def wA(s, c, half, kc=KC):
            n = SLOT // kc
            return ring[:, s % SLOTS, c * n + half * P:c * n + half * P + P]

        def wB(s, c, lo, n, kc=KC, width=None):
            w = width or SLOT // kc
            return ring[:, s % SLOTS, c * w + lo:c * w + lo + n]

        mods = S(6 * KC, 2)
        mulx, mulc = S(KC), S(KC)
        mul2 = S(KC)
        beta = S(2, 4, H1)
        gt = S(2, 4, H1)
        gc = S(2, 4, H1)
        eg = S(2, 4, H1)
        ed = S(2, 4, H1)
        et = S(2, 4, H1)
        beg = S(2, 4, H1)
        gtmp, gtmp2 = S(4, 8), S(4, 8)
        nega = S(8)
        posf = S(TT)
        ang, angk, cosx, sinx = S(TT, N_FREQ), S(TT, N_FREQ), S(TT, N_FREQ), S(TT, N_FREQ)
        logits = S(TT, 36)
        r4a, r4b, r8a, r8b, r8c = S(TT, 4), S(TT, 4), S(TT, 8), S(TT, 8), S(TT, 8)
        elp = S(TT, 32)
        r1v = S(7, TT)
        comb, routed, rank = S(TT, 32), S(TT, 32), S(TT, 32)
        load, rounds_f = S(32), S(4)
        graw = S(4, 16)
        mx, nmx, rsum, rinv = S(2, 4), S(2, 4), S(2, 4), S(2, 4)
        lam_p, lam_s, nlam = S(2, 32), S(4), S(2)
        st8, st8b = S(8), S(8)

        def A(at, *dims):
            return view(arena, at, *dims)

        ctxT = A(0, KC, T)
        gate_w = PR("wgates", KC, 16)
        hA = A(2048, KC, 2 * T)
        sqA = A(6144, KC, 2 * T)
        rsA = A(10240, 2 * T)
        silu_c = A(12960, KC, 32)
        modrow = A(13216, 3, T)
        padx = A(6144, 12, (GRID_R + 2) * PW)
        padc = A(10896, 8, T + 2)
        vT = A(0, H1, 2 * T)
        qT = A(12960, H1, T)
        kT = A(13984, H1, 2 * T)
        zT = A(16032, H1, T)
        ft = A(17056, TT, 512)
        sqq, sqk = A(6144, H1, T), A(7168, H1, 2 * T)
        rsk, rsq = sqk, sqq
        dftT = A(2048, TT, 2 * T)
        dftG = A(3072, 2, 2 * T)
        catF, oT = A(18080, H1, T), A(17056, H1, T)
        bM, bC, bD, bT, bU, bA, bQ, bS, bV = [A(2048 + 1024 * n, 2, H1, P) for n in range(9)]
        sqo = A(2048, H1, T)
        rso = A(3072, H1, T)
        h2 = A(0, KC, T)
        sq = A(2048, KC, T)
        rs = A(4096, 2 * T)
        h2tok = A(12160, TT, D)
        zeros = A(6656, 640)
        sel, selw = A(7296, TT, 2, SLOTN), A(7552, TT, 2, SLOTN)
        selT = A(7808, T)
        hG = A(8064, KC, 2 * SLOTN)
        hidT = A(9088, 4, 2 * SLOTN)
        ytok = A(10112, KC, P)
        sg, hid = A(11136, 512), A(11648, 512)
        h = h2
        memN = A(4608, KC, T)
        memsq = A(14208, KC, T)
        cat = A(6656, KC, T)
        yb = A(8704, KC, T)
        cv = A(8704, 5, T)
        krt = A(9984, TT, 32)
        zt = A(10048, TT, 512)
        dt_ = A(11072, TT, 768)
        qt = A(12608, TT, 768)
        kc = A(14144, TT, 768)
        vt = A(15680, TT, 512)
        QT, KT = A(0, MLA_H, T), A(2048, MLA_H, T)
        rtmp = A(16704, 4, TT * 8 * 16)
        rtk = A(17728, 4, TT * 16)
        Pb = [A(16704, TT, T), A(17216, TT, T), A(13120, TT, T), A(13632, TT, T)]
        PTb = [A(17728, TT, T), A(18240, TT, T)]
        ot = A(18752, TT, 256)
        dqT, dkT = A(8704, 2, T), A(9216, 2, T)
        ob = A(12608, TT, 256)
        sguw = A(14144, 4, P)
        memn = A(14656, KC, T)
        vm = A(10752, TT, D)
        qm = A(12800, KC, T)
        km = A(6656, KC, T)
        cat2, yb2 = A(8704, KC, T), A(6656, KC, T)
        ca = A(8704, 2, 4, T)
        fT = A(10752, 2, 2, T)

        ld_par, ld_cst, ld_x, ld_mem, ld_dft, ld_sgu, out_done = [
            sem(n) for n in ("ld_par", "ld_cst", "ld_x", "ld_mem", "ld_dft", "ld_sgu", "out_done")]
        full = [sem(f"slot_full{i}") for i in range(SLOTS)]
        free = sem("slots_free")
        v_step, a_step, zeroed = sem("v_step"), sem("a_step"), sem("zeroed")
        sq_ok, ss_ps, h_ok, x_ok = sem("sq_ok"), sem("ss_ps"), sem("h_ok"), sem("x_ok")
        root_ok = sem("root_ok")
        silu_0, silu_c_ok, mod_ps, mods_ok = sem("silu_0"), sem("silu_c_ok"), sem("mod_ps"), sem("mods_ok")
        modrow_ok, modt_ps = sem("modrow_ok"), sem("modt_ps")
        proj_ps, proj_ev = sem("proj_ps"), sem("proj_ev")
        conv_ok, act_ok = sem("conv_ok"), sem("act_ok")
        l2_sq, l2_ps, l2_ok = sem("l2_sq"), sem("l2_ps"), sem("l2_ok")
        gate_v, gate_a, gate_ps = sem("gate_v"), sem("gate_a"), sem("gate_ps")
        four_ps, four_g, four_cat = sem("four_ps"), sem("four_g"), sem("four_cat")
        gdn = {n: sem("gdn_" + n) for n in ("rows", "neg", "cm", "dd", "dn", "gb", "kk", "pre", "exp", "eq", "m", "ct", "u", "uc", "vv", "d",
                                            "tr", "tok", "nw", "nwc", "vn", "vnc", "st", "S")}
        gdn_start = sem("gdn_start")
        o_sq, o_ps, o_ok = sem("o_sq"), sem("o_ps"), sem("o_ok")
        rt_ps, rt_v, rt_a, rt_w = sem("rt_ps"), sem("rt_v"), sem("rt_a"), sem("rt_w")
        gu_ps, sg_ok, hid_ok, moe_ps = sem("gu_ps"), sem("sg_ok"), sem("hid_ok"), sem("moe_ps")
        tok_ps, rank_ps, zeros_ok, rounds_ok = sem("tok_ps"), sem("rank_ps"), sem("zeros_ok"), sem("rounds_ok")
        sel_ok, swt_ok, g_ps, hG_ok = sem("sel_ok"), sem("swt_ok"), sem("g_ps"), sem("hG_ok")
        y_ps, ylow_ok, tr_ps, yhigh_ok = sem("y_ps"), sem("ylow_ok"), sem("tr_ps"), sem("yhigh_ok")
        hidT_ok, selT_ok = sem("hidT_ok"), sem("selT_ok")
        rank_dn = sem("rank_dn")
        full2 = [sem(f"slot_full_late{i}") for i in range(SLOTS)]
        free2 = sem("slots_free_late")
        rope_v, rope_a = sem("rope_v"), sem("rope_a")
        mem_sq, mem_ok = sem("mem_sq"), sem("mem_ok")
        qk_ok, tq_ps, tq_ev = sem("qk_ok"), sem("tq_ps"), sem("tq_ev")
        sc_ps, max_ok, exp_ok, p_ok, pt_ps, pt_ev, o2_ps, o2_ev = [
            sem("at_" + n) for n in ("sc", "max", "exp", "p", "pt", "ptev", "o", "oev")]
        ln_ok, mix_ps, ob_ok = sem("ln_ok"), sem("mix_ps"), sem("ob_ok")
        ot_ok, tc_ps, cat_ok = sem("ot_ok"), sem("tc_ps"), sem("cat_ok")
        memn_ok = sem("memn_ok")
        up_ps, tap_ok, conv2_ok, gelu_ok, f_ok, ffn_ps, y_ok = [
            sem("ffn_" + n) for n in ("up", "tap", "conv", "gelu", "f", "y", "yev")]

        block = ctx.enter_context(nc.Block())

        @block.sync
        def _(sp):
            sp.dma_start(par[:, :], par_d).then_inc(ld_par, 16)
            sp.dma_start(cst[:, :], cst_d).then_inc(ld_cst, 16)
            sp.dma_start(row[:, :], row_d).then_inc(ld_cst, 16)
            for n in range(SLOTS):
                sp.dma_start(ring[:, n, :], stream[n]).then_inc(full[n], 16)
            for n in range(SLOTS, S_PRE):
                sp.wait_ge(free, n - SLOTS + 1)
                sp.dma_start(ring[:, n % SLOTS, :], stream[n]).then_inc(full[n % SLOTS], 16)
            with sp.Fori(0, PAIRS) as i:
                for j in range(SLOTS):
                    n = S_PRE + j
                    sp.wait_ge(free, i * SLOTS + (n - SLOTS + 1))
                    sp.dma_start(ring[:, n % SLOTS, :], stream[i * SLOTS + n]).then_inc(full[n % SLOTS], 16)
            sp.wait_ge(rounds_ok, 1)
            rounds = sp.value_load(rounds_i[0:1, 0:1], min_val=1, max_val=T // SLOTN)
            with sp.If(rounds > 1):
                with sp.Fori(1, rounds) as r:
                    with sp.Fori(0, PAIRS) as i:
                        for j in range(SLOTS):
                            n = S_PRE + j
                            sp.wait_ge(free, r * S_MOE + i * SLOTS + (n - SLOTS + 1))
                            sp.dma_start(ring[:, n % SLOTS, :], stream[i * SLOTS + n]).then_inc(full[n % SLOTS], 16)
            for j in range(SLOTS):
                n = S_PRE + j
                sp.wait_ge(free, rounds * S_MOE + (n - SLOTS + 1))
                sp.dma_start(ring[:, n % SLOTS, :], stream[n + S_MOE]).then_inc(full2[n % SLOTS], 16)
            n2 = S_LAYER * LAYERS
            with sp.Fori(0, n2 // SLOTS - 1) as r:
                for j in range(SLOTS):
                    n = S_PRE + j
                    sp.wait_ge(free2, r * SLOTS + (j + 1))
                    sp.dma_start(ring[:, n % SLOTS, :], stream[r * SLOTS + (n + S_MOE + SLOTS)])\
                        .then_inc(full2[n % SLOTS], 16)
            for m in range(n2 // SLOTS * SLOTS, n2):
                n = S_PRE + m
                sp.wait_ge(free2, m - SLOTS + 1)
                sp.dma_start(ring[:, n % SLOTS, :], stream[n + S_MOE]).then_inc(full2[n % SLOTS], 16)

        @block.gpsimd
        def _(pool):
            pool.wait_ge(h_ok, 1)
            nc.gpsimd.memset(arena[:, 6144:12960], 0.0).then_inc(zeroed, 1)

            def tt(out, a, b, op=ALU.mult):
                return nc.gpsimd.tensor_tensor(out, a, b, op)

            pool.wait_ge(gdn_start, 1)
            for s in range(4):
                tiles = (s, s ^ 1)
                full_h = [P, H1, P]
                for d in range(2):
                    if s:
                        pool.wait_ge(gdn["vn"], 2 * s - 1 + d)
                    tt(bD[:, d], over(C(f"cum{d}"), full_h), over(gt[:, d, tiles[d], :], full_h, 2))\
                        .then_inc(gdn["rows"], 1)
                    tt(bU[:, d], over(ident, full_h), over(beta[:, d, tiles[d], :], full_h, 2))\
                        .then_inc(gdn["rows"], 1)
                for d in range(2):
                    if s:
                        pool.wait_ge(gdn["st"], 2 * s - 1 + d)
                    elif d == 0:
                        pool.wait_ge(four_cat, 4)
                    tt(bC[:, d], over(C(f"neg{d}"), full_h), over(gc[:, d, tiles[d], :], full_h, 2), ALU.subtract)\
                        .then_inc(gdn["neg"], 1)
                for v in range(1, len(LEVELS)):
                    for d in range(2):
                        if v == 1:
                            pool.wait_ge(gdn["d"], 14 * s + d + 1)
                        else:
                            pool.wait_ge(gdn["u"], 14 * s + 2 * (v - 1) + d + 1)
                        tt(bC[:, d], bM[:, d], over(C(f"lev{d}", 7, P)[:, v, :], full_h)).then_inc(gdn["cm"], 1)

        def new_step(eng, step):
            n = [0]

            def link(ins):
                n[0] += 1
                ins.then_inc(step, 1)
                eng.wait_ge(step, n[0])
            return link

        def new_signal(eng):
            counts = {}

            def signal(ins, s, wait=True):
                counts[s.name] = counts.get(s.name, 0) + 1
                ins.then_inc(s, 1)
                if wait:
                    eng.wait_ge(s, counts[s.name])
                return counts[s.name]
            return signal

        @block.tensor
        def _(pe):
            pend = [0]
            pos = [0]
            late = [False]
            jobs = [0]

            def mm(out, lhsT, rhs, start=True, stop=True, inc=None, tr=False, skip=False):
                if tr:
                    i = nc.tensor.transpose(out, lhsT, rhs)
                else:
                    i = nc.tensor.matmul(out, lhsT, rhs, start=start, stop=stop, skip_group_check=skip)
                if inc is not None:
                    i.then_inc(inc, 1)
                elif pend[0]:
                    i.then_inc(free2 if late[0] else free, pend[0])
                    pend[0] = 0
                return i

            def arrive():
                n = pos[0]
                if late[0]:
                    pe.wait_ge(full2[n % SLOTS], 16 * ((n - S_PRE) // SLOTS + 1))
                else:
                    pe.wait_ge(full[n % SLOTS], 16 * (n // SLOTS + 1))
                pos[0] += 1
                return n

            def release():
                pend[0] += 1

            def job_bank():
                j = jobs[0]
                if j >= 4:
                    pe.wait_ge(proj_ev, j - 3)
                jobs[0] += 1
                return j % 4

            def job_a(s, half, mov, n, kc=KC):
                out = bank(job_bank(), n)
                for c in range(kc):
                    mm(out, wA(s, c, half, kc), mov[:, c, :], c == 0, c == kc - 1,
                       proj_ps if c == kc - 1 else None)

            def job_b(s, src, t0, lo, n, tiles=1, kc=KC, width=None):
                b = job_bank()
                for t in range(tiles):
                    for c in range(kc):
                        last = c == kc - 1
                        mm(bank(b, tiles * n)[:, t * n:t * n + n], src[:, c, t0 + t * P:t0 + t * P + P],
                           wB(s, c, lo, n, kc, width), c == 0, last, proj_ps if last and t == tiles - 1 else None)

            norms = [0]

            def sum_squares(parts, n):
                norms[0] += 1
                pe.wait_ge(sq_ok, norms[0])
                if norms[0] > 1:
                    pe.wait_ge(h_ok, norms[0] - 1)
                for k, (v, chunks) in enumerate(parts):
                    for i, c in enumerate(chunks):
                        last = i == len(chunks) - 1
                        mm(bank(4, len(parts) * n)[:, k * n:k * n + n], ones, v[:, c, :], i == 0, last,
                           ss_ps if last and k == len(parts) - 1 else None)

            pe.wait_ge(ld_par, 16)
            pe.wait_ge(ld_cst, 32)
            sum_squares([(sqA, range(KC))], 2 * T)
            pe.wait_ge(silu_c_ok, 1)
            with pe.Fori(0, S_MOD // SLOTS) as r:
                for k in range(SLOTS // 4):
                    for q in range(4):
                        pe.wait_ge(full[4 * k + q], r * 16 + 16)
                    for c in range(KC):
                        for q in range(4):
                            i = nc.tensor.matmul(bank(k, T)[32 * q:32 * q + 32, :], silu_c[:, c, :],
                                                 wB(4 * k + q, c, 0, T), start=c == 0, stop=c == KC - 1,
                                                 tile_position=(0, 32 * q))
                            if c == KC - 1:
                                i.then_inc(free if q < 3 else mod_ps, 1)
                    pe.wait_ge(modrow_ok, r * 3 + k + 1)
                    nc.tensor.transpose(bank(5, T)[:, 0:P], modrow[:, k, 0:P], ident).then_inc(free, 1)
                    nc.tensor.transpose(bank(5, T)[:, P:T], modrow[:, k, P:T], ident).then_inc(modt_ps, 1)
                    pe.wait_ge(mods_ok, r * 3 + k + 1)
            pos[0] = S_MOD

            pe.wait_ge(h_ok, 1)
            b = job_bank()
            for t in range(4):
                for c in range(KC):
                    mm(bank(b, 4, 16)[:, t, :], hA[:, c, t * P:t * P + P], gate_w[:, c, :], c == 0, c == KC - 1,
                       proj_ps if c == KC - 1 and t == 3 else None)
            for k in range(2):
                s = arrive()
                for t in range(TT):
                    job_b(s, hA, T + t * P, 0, T)
                release()
            for k in range(8):
                if k == 6:
                    pe.wait_ge(l2_sq, 1)
                    for hd in range(H1):
                        mm(bank(4 + hd, 2 * T), ones, sqk[:, hd, :], inc=l2_ps if hd == H1 - 1 else None)
                if k == 7:
                    pe.wait_ge(root_ok, 2)
                    for hd in range(H1):
                        mm(bank(4 + hd // 2, 2 * T)[:, hd % 2 * T:hd % 2 * T + T], ones, sqq[:, hd, :],
                           inc=l2_ps if hd == H1 - 1 else None)
                s = arrive()
                for half in range(2):
                    job_a(s, half, hA[:, :, T:2 * T] if k < 2 or k >= 6 else hA, T if k < 2 or k >= 6 else 2 * T)
                release()

            pe.wait_ge(gate_v, 2)
            gflat = gt.rearrange("p d t h -> p d (t h)")
            for d in range(2):
                mm(bank(6, 64)[:, 16 * d:16 * d + 16], C(f"cum{d}"), gflat[:, d, :])
            mm(bank(6, 64)[:, 32:64], ones, gt.rearrange("p d t h -> p (d t h)"), inc=gate_ps)

            pe.wait_ge(ld_dft, 16)
            pe.wait_ge(proj_ev, jobs[0])
            for g in range(4):
                for t in range(TT):
                    mm(bank(g % 2, 2 * T), ft[:, t, g * P:g * P + P], dftT[:, t, :], t == 0, t == 1,
                       four_ps if t == 1 else None)
                pe.wait_ge(four_g, g + 1)
                if g >= 2:
                    pe.wait_ge(four_cat, g - 1)
                for k in range(2):
                    mm(bank(2 + g % 2, T), view(cst, CST["dftc"][0] + k * P, P), dftG[:, g % 2, k * T:k * T + T],
                       k == 0, k == 1, four_ps if k == 1 else None)

            for s in range(4):
                tiles = (s, s ^ 1)
                xs = s >= 2

                def heads(b, lhsT, rhs, sig=None):
                    for hd in range(H1):
                        mm(bank(b, H1, P)[:, hd, :], lhsT(hd), rhs(hd), inc=sig if hd == H1 - 1 else None)

                if s == 0:
                    pe.wait_ge(four_cat, 4)
                    pe.wait_ge(l2_ok, 1)
                    pe.wait_ge(gate_v, 3)
                for d in range(2):
                    tk = slice(tiles[d] * P, tiles[d] * P + P)
                    tq = slice((tiles[d] - 2) * P, (tiles[d] - 2) * P + P)
                    heads(4 + d, lambda hd: kT[:, hd, tk], lambda hd: kT[:, hd, tk], None if xs else gdn["kk"])
                    pe.wait_ge(gdn["rows"], 4 * s + 2 * d + 2)
                    mm(bank(2 + d, 512), ones, bU[:, d].rearrange("p h i -> p (h i)"))
                    pe.wait_ge(gdn["S"], 2 * s + d + 1)
                    mm(bank(d, 512), ones, bD[:, d].rearrange("p h i -> p (h i)"), inc=gdn["gb"])
                    if xs:
                        heads(6 + d, lambda hd: kT[:, hd, tk], lambda hd: qT[:, hd, tq], gdn["kk"])
                for d in range(2):
                    pe.wait_ge(gdn["ct"], 2 * s + d + 1)
                    for hd in range(H1):
                        mm(bank(d, H1, P)[:, hd, :], bC[:, d, hd, :], ident, tr=True,
                           inc=gdn["u"] if hd == H1 - 1 else None)
                for v in range(1, len(LEVELS)):
                    for d in range(2):
                        pe.wait_ge(gdn["cm"], 12 * s + 2 * (v - 1) + d + 1)
                        if v == 1:
                            pe.wait_ge(gdn["d"], 14 * s + d + 1)
                        else:
                            pe.wait_ge(gdn["dn"], 10 * s + 2 * (v - 2) + d + 1)
                        heads(d, lambda hd: bC[:, d, hd, :], lambda hd: bD[:, d, hd, :], gdn["u"])
                    for d in range(2):
                        pe.wait_ge(gdn["uc"], 12 * s + 2 * (v - 1) + d + 1)
                        pe.wait_ge(gdn["d"], 14 * s + 2 * (v - 1) + d + 1)
                        if v < len(LEVELS) - 1:
                            heads(2 + d, lambda hd: bT[:, d, hd, :], lambda hd: bU[:, d, hd, :], gdn["dd"])
                        heads(4 + d, lambda hd: bU[:, d, hd, :], lambda hd: bT[:, d, hd, :], gdn["vv"])
                for d in range(2):
                    for hd in range(H1):
                        mm(bank(d, H1, P)[:, hd, :], kT[:, hd, tiles[d] * P:tiles[d] * P + P], ident, tr=True)
                    for hd in range(H1):
                        mm(bank(6 + d, H1, P)[:, hd, :], vT[:, hd, tiles[d] * P:tiles[d] * P + P], ident, tr=True,
                           inc=gdn["tr"] if hd == H1 - 1 else None)
                for d in range(2):
                    pe.wait_ge(gdn["d"], 14 * s + 12 + d + 1)
                    pe.wait_ge(gdn["tok"], 2 * s + d + 1)
                    heads(2 + d, lambda hd: bM[:, d, hd, :], lambda hd: bT[:, d, hd, :], gdn["nw"])
                for d in range(2):
                    pe.wait_ge(gdn["nwc"], 2 * s + d + 1)
                    pe.wait_ge(gdn["S"], 2 * s + d + 1)
                    for hd in range(H1):
                        mm(bank(4 + d, H1, P)[:, hd, :], bT[:, d, hd, :], bD[:, d, hd, :], True, False)
                        mm(bank(4 + d, H1, P)[:, hd, :], bU[:, d, hd, :], bS[:, d, hd, :], False, True,
                           inc=gdn["vn"] if hd == H1 - 1 else None)
                for d in range(2):
                    pe.wait_ge(gdn["vnc"], 2 * s + d + 1)
                    if xs:
                        for hd in range(H1):
                            mm(bank(6 + d, H1, P)[:, hd, :], bS[:, d, hd, :], bQ[:, d, hd, :], True, False)
                            mm(bank(6 + d, H1, P)[:, hd, :], bV[:, d, hd, :], bA[:, d, hd, :], False, True)
                    heads(d, lambda hd: bC[:, d, hd, :], lambda hd: bV[:, d, hd, :], gdn["st"])

            pe.wait_ge(o_sq, 1)
            for k in range(2):
                mm(bank(2 + k, 512), ones, sqo[:, 2 * k:2 * k + 2, :].rearrange("p h t -> p (h t)"),
                   inc=o_ps if k else None)

            pe.wait_ge(o_ok, 1)
            for k in range(S_OUT):
                s = arrive()
                for half in range(2):
                    b = job_bank()
                    for c in range(KC):
                        mm(bank(b, T), wA(s, c, half), catF[:, c, :] if c < 4 else oT[:, c - 4, :], c == 0, c == KC - 1,
                           proj_ps if c == KC - 1 else None)
                release()

            sum_squares([(sq, range(KC))], T)
            pe.wait_ge(mem_sq, 1)
            for c in range(KC):
                mm(bank(5, T), ones, memsq[:, c, :], c == 0, c == KC - 1, inc=moe_ps if c == KC - 1 else None)
            pe.wait_ge(h_ok, norms[0])
            rw = PR("wroute", KC, 36)
            b = job_bank()
            for t in range(TT):
                for c in range(KC):
                    mm(bank(b, TT, 36)[:, t, :], h2[:, c, t * P:t * P + P], rw[:, c, :], c == 0, c == KC - 1,
                       proj_ps if c == KC - 1 and t == 1 else None)
            pe.wait_ge(proj_ev, jobs[0])
            for t in range(TT):
                for c in range(KC):
                    mm(bank(2 * t, KC, P)[:, c, :], h2[:, c, t * P:t * P + P], ident, tr=True,
                       inc=tok_ps if c == KC - 1 else None)
            pe.wait_ge(zeros_ok, 1)
            mm(bank(6, 96)[:, 0:32], C("cum0"), routed[:, 0, :])
            mm(bank(6, 96)[:, 32:64], C("cum0"), routed[:, 1, :], True, False)
            mm(bank(6, 96)[:, 32:64], ones, routed[:, 0, :], False, True)
            mm(bank(6, 96)[:, 64:96], ones, routed[:, 0, :], True, False)
            mm(bank(6, 96)[:, 64:96], ones, routed[:, 1, :], False, True, inc=rank_ps)
            pe.wait_ge(hG_ok, 2)
            pe.wait_ge(rounds_ok, 1)
            for b in range(4):
                mm(bank(4 + b, 512), zeros[:, 0:P], zeros[:, P:640], True, False, skip=True)
            assert pos[0] == S_PRE and not pend[0]
            rounds = pe.value_load(rounds_i[0:1, 0:1], min_val=1, max_val=T // SLOTN)
            with pe.Fori(0, rounds) as r:
                with pe.Fori(0, PAIRS) as i:
                    def at(k, c):
                        return r * (PAIRS * k) + i * k + c

                    def arrive_moe(j):
                        n = S_PRE + j
                        pe.wait_ge(full[n % SLOTS], r * (16 * PAIRS) + i * 16 + 16 * (n // SLOTS + 1))
                        return n

                    pe.wait_ge(sel_ok, at(1, 1))
                    for c in range(KC):
                        for t in range(TT):
                            mm(bank(0, KC, P)[:, c, :], h2tok[:, t, c * P:c * P + P],
                               sel[:, t].rearrange("p e n -> p (e n)"), t == 0, t == 1,
                               inc=g_ps if c % 4 == 3 and t else None)
                    pe.wait_ge(hG_ok, at(2, 3))
                    for j in range(4):
                        n = [arrive_moe(2 * j + e) for e in range(2)]
                        for c in range(KC):
                            if j == 0 and c == 4:
                                pe.wait_ge(hG_ok, at(2, 4))
                            for e in range(2):
                                last = c == KC - 1
                                mm(bank(2 + j % 2, 512)[e * SLOTN:e * SLOTN + SLOTN, j // 2 * T:j // 2 * T + T],
                                   hG[:, c, e * SLOTN:e * SLOTN + SLOTN], wB(n[e], c, 0, T), c == 0, last,
                                   gu_ps if last and e and j == 3 else None)
                        for e in range(2):
                            release()
                    pe.wait_ge(swt_ok, at(1, 1))
                    for t in range(TT):
                        mm(bank(1, T)[:, t * P:t * P + P], selw[:, t].rearrange("p e n -> p (e n)"), ident, tr=True)
                    pe.wait_ge(hid_ok, at(1, 1))
                    for k in range(4):
                        mm(bank(0, 4, P)[:, k, :], hid[:, k * P:k * P + P], ident, tr=True,
                           inc=tr_ps if k == 3 else None)
                    pe.wait_ge(hidT_ok, at(1, 1))
                    for o in range(2):
                        n = [arrive_moe(8 + 2 * o + e) for e in range(2)]
                        for k in range(4):
                            for e in range(2):
                                mm(bank(2 + o, 512)[e * SLOTN:e * SLOTN + SLOTN, :],
                                   hidT[:, k, e * SLOTN:e * SLOTN + SLOTN], wB(n[e], k, 0, 512, 4), k == 0, k == 3,
                                   y_ps if e and k == 3 else None)
                        for e in range(2):
                            release()
                    pe.wait_ge(selT_ok, at(1, 1))
                    pe.wait_ge(ylow_ok, at(1, 1))
                    for o in range(KC):
                        if o == 4:
                            pe.wait_ge(yhigh_ok, at(1, 1))
                        mm(bank(4 + o // 2, 2, T)[:, o % 2, :], ytok[:, o, :], selT, False, False, skip=True)
                    assert not pend[0]
            pos[0] = S_PRE
            late[0] = True
            mm(bank(0, 1), ident, ident[:, 0:1], inc=moe_ps)
            sum_squares([(sq, range(KC))], T)

            for l in range(LAYERS):
                sum_squares([(sq, range(KC))], T)
                pe.wait_ge(h_ok, norms[0])
                h_ready = [norms[0]]
                for k in range(8):
                    s = arrive()
                    if k < 3:
                        for half in range(2 if k < 2 else 1):
                            job_a(s, half, h, T)
                        if k == 2:
                            job_b(s, h, 0, P, 32, tiles=2)
                    else:
                        job_b(s, h, 0, 0, T, tiles=2)
                    release()
                sum_squares([(sq, range(3)), (sq, range(3, 5))], T)
                pe.wait_ge(h_ok, norms[0])
                for k in range(2):
                    s = arrive()
                    for t in range(TT):
                        job_b(s, cv, t * P, 0, 384, kc=3, width=384)
                    release()
                s = arrive()
                for t in range(TT):
                    for n in range(2):
                        job_b(s, cv[:, 3:5, :], t * P, n * 512, 512, kc=2, width=1024)
                release()
                tq0 = 10 * l
                for k in range(10):
                    if k >= 4:
                        pe.wait_ge(tq_ev, tq0 + k - 3)
                    if k == 0:
                        pe.wait_ge(qk_ok, 3 * l + 1)
                    if k == 4:
                        pe.wait_ge(qk_ok, 3 * l + 2)
                    if k == 8:
                        pe.wait_ge(qk_ok, 3 * l + 3)
                    if k < 8:
                        src = qt if k < 4 else kc
                        for hh in range(2):
                            hd = 2 * (k % 4) + hh
                            for t in range(TT):
                                mm(bank(4 + k % 4, 2, T)[0:MLA_D, hh, t * P:t * P + P],
                                   src[:, t, hd * MLA_D:hd * MLA_D + MLA_D], ident, tr=True,
                                   inc=tq_ps if hh and t else None)
                    else:
                        for c in range(2):
                            for t in range(TT):
                                mm(bank(4 + k % 4, 2, T)[:, c, t * P:t * P + P],
                                   dt_[:, t, (k - 8) * 256 + c * P:(k - 8) * 256 + c * P + P], ident, tr=True,
                                   inc=tq_ps if c and t else None)
                pe.wait_ge(tq_ev, tq0 + 10)

                def scores(g, q, u):
                    if g >= 2:
                        pe.wait_ge(exp_ok, g - 1)
                    for c in range(2 if 8 <= u < 12 else 1):
                        for t in range(TT):
                            o = bank(2 * q + c, TT, T)[:, t, :]
                            last = t == 1 and (c == 1 or not 8 <= u < 12)
                            if u < 8:
                                mm(o, QT[0:MLA_D, u, t * P:t * P + P], KT[0:MLA_D, u, :], inc=sc_ps if last else None)
                            elif u < 12:
                                r = 64 * (u % 2) + 32 * c
                                mm(o, dqT[r:r + 32, (u - 8) // 2, t * P:t * P + P], dkT[r:r + 32, (u - 8) // 2, :],
                                   inc=sc_ps if last else None)
                            else:
                                for dc in range(2):
                                    mm(o, qm[:, 2 * (u - 12) + dc, t * P:t * P + P], km[:, 2 * (u - 12) + dc, :],
                                       dc == 0, dc == 1, inc=sc_ps if last and dc else None)

                def values(g, q, u):
                    pe.wait_ge(p_ok, g + 1)
                    if g >= 2:
                        pe.wait_ge(pt_ev, g - 1)
                    for kt in range(TT):
                        for t in range(TT):
                            mm(bank(4 + q, TT, T)[:, kt, t * P:t * P + P], Pb[q][:, t, kt * P:kt * P + P], ident,
                               tr=True, inc=pt_ps if kt and t else None)
                    pe.wait_ge(pt_ev, g + 1)
                    if g >= 2:
                        pe.wait_ge(o2_ev, g - 1)
                    for k in range(1 if u < 8 else 2):
                        for kt in range(TT):
                            if u < 8:
                                r = 64 * (u % 2)
                                mm(bank(6 + q, T)[r:r + 64, :], vt[:, kt, u * 64:u * 64 + 64], PTb[q][:, kt, :],
                                   kt == 0, kt == 1, inc=o2_ps if kt else None)
                            elif u < 12:
                                mm(bank(6 + q, TT, 64)[:, k, :], PTb[q][:, kt, k * P:k * P + P],
                                   dt_[:, kt, 512 + (u - 8) * 64:512 + (u - 8) * 64 + 64],
                                   kt == 0, kt == 1, inc=o2_ps if kt and k else None)
                            else:
                                mm(bank(6 + q, TT, T)[:, k, :],
                                   vm[:, kt, (u - 12) * 256 + k * P:(u - 12) * 256 + k * P + P], PTb[q][:, kt, :],
                                   kt == 0, kt == 1, inc=o2_ps if kt and k else None)

                def attention(units):
                    scores(16 * l + units[0], units[0] % 2, units[0])
                    for u in units:
                        if u + 1 in units:
                            scores(16 * l + u + 1, (u + 1) % 2, u + 1)
                        values(16 * l + u, u % 2, u)

                attention(range(12))
                pe.wait_ge(o2_ev, 16 * l + 12)
                pe.wait_ge(ld_sgu, 16 * (l + 1))
                for t in range(TT):
                    for g in range(4):
                        mm(bank(4, TT * 4, 64)[:, 4 * t + g, :], sguw[:, g, :], zt[:, t, 256 + 64 * g:256 + 64 * g + 64],
                           inc=mix_ps if t and g == 3 else None)
                for k in range(2):
                    pe.wait_ge(ot_ok, 2 * l + k + 1)
                    src = ob if k == 0 else ot
                    for c in range(2):
                        for t in range(TT):
                            mm(bank(6 + k, 2, T)[:, c, t * P:t * P + P], src[:, t, c * P:c * P + P], ident, tr=True,
                               inc=tc_ps if c and t else None)
                pe.wait_ge(cat_ok, 2 * l + 2)
                for k in range(4):
                    s = arrive()
                    for half in range(2):
                        job_a(s, half, cat, T)
                    release()

                def mem_kv(slots):
                    for k in slots:
                        s = arrive()
                        if k < 4:
                            for half in range(2):
                                job_a(s, half, memn, T)
                        else:
                            job_b(s, memn, 0, 0, T, tiles=2)
                        release()

                pe.wait_ge(memn_ok, l + 1)
                mem_kv(range(2))
                sum_squares([(sq, range(KC))], T)
                mem_kv(range(2, 4))
                sum_squares([(sq, range(KC))], T)
                mem_kv(range(4, 8))
                pe.wait_ge(h_ok, norms[0])
                for k in range(4):
                    s = arrive()
                    for half in range(2):
                        job_a(s, half, h, T)
                    release()
                pe.wait_ge(proj_ev, jobs[0])
                attention(range(12, 16))
                pe.wait_ge(o2_ev, 16 * l + 16)
                for k in range(4):
                    s = arrive()
                    for half in range(2):
                        job_a(s, half, cat2, T)
                    release()
                sum_squares([(sq, range(KC))], T)
                sum_squares([(sq, range(KC))], T)
                pe.wait_ge(h_ok, norms[0])

                def up(i):
                    f = FFN_PAIRS * l + i
                    if f >= 2:
                        pe.wait_ge(f_ok, f - 1)
                    for w in range(2):
                        s = arrive()
                        for half in range(2):
                            for c in range(KC):
                                last = c == KC - 1
                                mm(bank(2 * (f % 2) + w, 2, T)[:, half, :], wA(s, c, half), h[:, c, :], c == 0, last,
                                   up_ps if last and half and w else None)
                        release()

                def down(i):
                    f = FFN_PAIRS * l + i
                    s = arrive()
                    pe.wait_ge(f_ok, f + 1)
                    for o in range(KC):
                        for k in range(2):
                            mm(bank(4 + o // 2, 2, T)[:, o % 2, :],
                               ring[:, s % SLOTS, k * 1024 + o * P:k * 1024 + o * P + P], fT[:, f % 2, k, :],
                               i == 0 and k == 0 and o % 2 == 0, False, skip=True,
                               inc=ffn_ps if i == FFN_PAIRS - 1 and k and o == KC - 1 else None)
                    release()

                up(0)
                for i in range(FFN_PAIRS):
                    if i + 1 < FFN_PAIRS:
                        up(i + 1)
                    down(i)
                pe.wait_ge(y_ok, l + 1)
                sum_squares([(sq, range(KC))], T)

        @block.scalar
        def _(act):
            act.dma_start(ctxT, xc_d[0]).then_inc(ld_x, 16)
            act.dma_start(xT[:, :, :], xc_d[1]).then_inc(ld_x, 16)
            act.dma_start(ipos[:, :], pos_d).then_inc(ld_x, 16)
            A_ = nc.scalar.activation
            signal = new_signal(act)
            jobs, norms = [0], [0]

            def take():
                act.wait_ge(proj_ps, jobs[0] + 1)
                jobs[0] += 1
                return (jobs[0] - 1) % 4

            def evac(dst, src, fn=ACT.Copy, done=True):
                i = A_(dst, src, fn)
                if done:
                    i.then_inc(proj_ev, 1)

            def squares(dst, src, after=None):
                norms[0] += 1
                if after is not None:
                    act.wait_ge(h_ok, after)
                A_(dst, src, ACT.Square).then_inc(sq_ok, 1)

            def evac_squares(y):
                norms[0] += 1
                for j in range(KC):
                    b = take()
                    i = A_(sq[:, j, :], bank(b, T), ACT.Square)
                    if j == KC - 1:
                        i.then_inc(sq_ok, 1)
                    evac(y[:, j, :], bank(b, T))

            def root(dst, src, n):
                return A_(dst, src, ACT.Sqrt, scale=1.0 / n, bias=EPS)

            def norm_root(dst=rs[:, 0:T]):
                act.wait_ge(ss_ps, norms[0])
                root(dst, bank(4, T), D).then_inc(root_ok, 1)

            act.wait_ge(ld_par, 16)
            act.wait_ge(silu_0, 1)
            A_(silu_c[:, :, 0:2], PR("c", KC, 2), ACT.Silu).then_inc(silu_c_ok, 1)
            act.wait_ge(ld_cst, 32)
            act.wait_ge(ld_x, 48)
            A_(sqA[:, :, 0:T], ctxT, ACT.Square)
            squares(sqA[:, :, T:2 * T], xT[:, :, :])
            act.wait_ge(ss_ps, 1)
            root(rsA, bank(4, 2 * T), D).then_inc(root_ok, 1)
            act.wait_ge(rope_v, 1)
            A_(sinx, angk, ACT.Sin)
            A_(cosx, ang, ACT.Sin).then_inc(rope_a, 1)
            act.wait_ge(rope_v, 2)
            A_(lam_s, lam_s, ACT.Exp)
            A_(nega, RW("alog"), ACT.Exp).then_inc(rope_a, 1)

            with act.Fori(0, S_MOD // SLOTS) as r:
                for k in range(SLOTS // 4):
                    act.wait_ge(mod_ps, r * 3 + k + 1)
                    A_(modrow[:, k, :], bank(k, T), ACT.Copy).then_inc(modrow_ok, 1)

            b = take()
            evac(graw.rearrange("p t k -> p (t k)"), bank(b, 64))
            act.wait_ge(proj_ev, 1)
            A_(beta.rearrange("p d t h -> p t d h"), graw[:, :, 0:8].rearrange("p t (d h) -> p t d h", d=2),
               ACT.Sigmoid).then_inc(gate_a, 1)
            act.wait_ge(gate_v, 1)
            signal(A_(gtmp2, gtmp2, ACT.Exp, scale=-1.0), a_step)
            A_(gtmp2, gtmp2, ACT.Ln, bias=1.0).then_inc(gate_a, 1)

            for k in range(2):
                for t in range(TT):
                    b = take()
                    evac(ft[:, t, k * T:k * T + T], bank(b, T))
            act.wait_ge(zeroed, 1)

            def smooth(j):
                act.wait_ge(conv_ok, j + 1)
                v = qT[:, j, :] if j < 4 else kT[:, j - 4, :] if j < 8 else vT[:, j - 8, :]
                A_(v, v, ACT.Silu).then_inc(act_ok, 1)

            for j in range(16):
                b = take()
                if j < 12:
                    grid = padx[:, j, :].rearrange("p (r c) -> p r c", c=PW)[:, 1:1 + GRID_R, 1:1 + GRID_W]
                    src = bank(b, T) if j < 4 else bank(b, 2 * T)
                    if j >= 4:
                        evac(padc[:, j - 4, 1:1 + T], src[:, 0:T], done=False)
                        src = src[:, T:2 * T]
                    evac(grid, src.rearrange("p (r c) -> p r c", c=GRID_W))
                else:
                    evac(zT[:, j - 12, :], bank(b, T), ACT.Silu)
                if 2 <= j < 14:
                    smooth(j - 2)
                if j == 9:
                    act.wait_ge(act_ok, 8)
                    A_(sqk, kT, ACT.Square)
                    A_(sqq, qT, ACT.Square).then_inc(l2_sq, 1)
                if j == 12:
                    act.wait_ge(l2_ps, 1)
                    root(rsk.rearrange("p h t -> p (h t)"), bank(4, 8 * T), 1).then_inc(root_ok, 1)
                if j == 14:
                    act.wait_ge(l2_ps, 2)
                    root(rsq.rearrange("p h t -> p (h t)"), bank(4, 4 * T), 1).then_inc(root_ok, 1)
            act.wait_ge(proj_ps, jobs[0])
            act.dma_start(dftT, dft_d).then_inc(ld_dft, 16)
            for g in range(4):
                act.wait_ge(four_ps, 2 * g + 1)
                A_(dftG[:, g % 2, :], bank(g % 2, 2 * T), ACT.Copy).then_inc(four_g, 1)
                act.wait_ge(four_ps, 2 * g + 2)
                A_(catF[:, g, :], bank(2 + g % 2, T), ACT.Copy).then_inc(four_cat, 1)
            act.wait_ge(gate_v, 3)
            A_(eg, gc, ACT.Exp)
            A_(ed, ed, ACT.Exp)
            A_(et, et, ACT.Exp).then_inc(gate_a, 1)
            for s in range(4):
                for d in range(2):
                    act.wait_ge(gdn["pre"], 2 * s + d + 1)
                    A_(bC[:, d], bC[:, d], ACT.Exp).then_inc(gdn["exp"], 1)
                    if s >= 2:
                        A_(bQ[:, d], bank(d, H1, P), ACT.Exp).then_inc(gdn["eq"], 1)
                for v in range(1, len(LEVELS)):
                    for d in range(2):
                        act.wait_ge(gdn["u"], 14 * s + 2 * v + d + 1)
                        A_(bU[:, d], bank(d, H1, P), ACT.Copy).then_inc(gdn["uc"], 1)
                for d in range(2):
                    act.wait_ge(gdn["nw"], 2 * s + d + 1)
                    A_(bU[:, d], bank(2 + d, H1, P), ACT.Copy, scale=-1.0).then_inc(gdn["nwc"], 1)
                for d in range(2):
                    act.wait_ge(gdn["vn"], 2 * s + d + 1)
                    A_(bV[:, d], bank(4 + d, H1, P), ACT.Copy).then_inc(gdn["vnc"], 1)
            act.wait_ge(gdn["S"], 10)
            A_(sqo, oT, ACT.Square).then_inc(o_sq, 1)
            act.wait_ge(o_ps, 1)
            root(rso.rearrange("p h t -> p (h t)"), bank(2, 4 * T), P).then_inc(root_ok, 1)
            for j in range(8):
                b = take()
                evac(yb[:, j, :], bank(b, T))
            act.wait_ge(x_ok, 1)
            act.dma_start(memN, mem_d).then_inc(ld_mem, 16)
            squares(sq, xT[:, :, :])
            norm_root()
            act.wait_ge(ld_mem, 16)
            A_(memsq, memN, ACT.Square).then_inc(mem_sq, 1)
            act.wait_ge(moe_ps, 1)
            root(rs[:, T:2 * T], bank(5, T), D).then_inc(root_ok, 1)
            b = take()
            evac(logits, bank(b, TT, 36))
            act.wait_ge(rt_v, 1)
            A_(r4a, r4a, ACT.Exp)
            A_(r1v[:, 2], r1v[:, 2], ACT.Exp).then_inc(rt_a, 1)
            for t in range(TT):
                act.wait_ge(tok_ps, t + 1)
                A_(h2tok[:, t, :], bank(2 * t, D), ACT.Copy).then_inc(hG_ok, 1)
            act.wait_ge(rounds_ok, 1)
            rounds = act.value_load(rounds_i[0:1, 0:1], min_val=1, max_val=T // SLOTN)
            with act.Fori(0, rounds) as r:
                with act.Fori(0, PAIRS) as i:
                    def at(k, c):
                        return r * (PAIRS * k) + i * k + c

                    for k in range(2):
                        act.wait_ge(g_ps, at(2, 1 + k))
                        A_(hG[:, 4 * k:4 * k + 4, :], bank(k, 4, P), ACT.Copy).then_inc(hG_ok, 1)
                    act.wait_ge(gu_ps, at(1, 1))
                    A_(sg, bank(2, 512), ACT.Silu).then_inc(sg_ok, 1)
                    act.wait_ge(tr_ps, at(1, 1))
                    A_(hidT, bank(0, 4, P), ACT.Copy).then_inc(hidT_ok, 1)
                    act.wait_ge(y_ps, at(2, 1))
                    A_(ytok[:, 0:4, :], bank(2, 4, P), ACT.Copy).then_inc(ylow_ok, 1)
            act.wait_ge(x_ok, 2)
            squares(sq, xT[:, :, :])
            norm_root()

            for l in range(LAYERS):
                n0 = 3 + 7 * l
                g0 = 16 * l
                squares(sq, xT[:, :, :], n0)
                norm_root()
                for j in range(5):
                    b = take()
                    evac(cv[:, j, :], bank(b, T))
                b = take()
                evac(krt, bank(b, TT, 32))
                act.wait_ge(proj_ev, jobs[0] - 1)
                squares(sq[:, 0:5, :], cv)
                for k in range(5):
                    b = take()
                    if k < 2:
                        evac(zt[:, :, k * T:k * T + T], bank(b, TT, T), ACT.Gelu_apprx_tanh)
                    else:
                        evac(dt_[:, :, (k - 2) * T:(k - 1) * T], bank(b, TT, T))
                act.wait_ge(ss_ps, norms[0])
                root(rs[:, 0:T], bank(4, T), 384)
                root(rs[:, T:2 * T], bank(4, 2 * T)[:, T:2 * T], 256).then_inc(root_ok, 1)
                act.wait_ge(ln_ok, 2 * l + 1)
                root(st8b, st8b, 64).then_inc(root_ok, 1)
                for k in range(2):
                    for t in range(TT):
                        b = take()
                        evac(qt[:, t, k * 384:k * 384 + 384], bank(b, 384))
                for t in range(TT):
                    for n in range(2):
                        b = take()
                        src = bank(b, 4, P)
                        evac(kc[:, t, n * 384:n * 384 + 384].rearrange("p (h d) -> p h d", h=4)[:, :, 0:64],
                             src[:, :, 0:64], done=False)
                        evac(vt[:, t, n * 256:n * 256 + 256].rearrange("p (h d) -> p h d", h=4), src[:, :, 64:128])
                for k in range(10):
                    act.wait_ge(tq_ps, 10 * l + k + 1)
                    src = bank(4 + k % 4, 2, T)
                    if k < 8:
                        dst = (QT if k < 4 else KT)[0:MLA_D, 2 * (k % 4):2 * (k % 4) + 2, :]
                        A_(dst, src[0:MLA_D], ACT.Copy).then_inc(tq_ev, 1)
                    else:
                        A_(dqT if k == 8 else dkT, src, ACT.Copy).then_inc(tq_ev, 1)
                act.dma_start(sguw, sguw_d[l]).then_inc(ld_sgu, 16)

                def exps(u):
                    g, q = g0 + u, u % 2
                    act.wait_ge(max_ok, g + 1)
                    scale = (MLA_D if u < 8 else 32 if u < 12 else 256) ** -0.5
                    n = 4 if 8 <= u < 12 else 2
                    for k in range(n):
                        i = A_(Pb[2 * (k // 2) + q][:, k % 2, :], bank(2 * q + k // 2, TT, T)[:, k % 2, :], ACT.Exp,
                               bias=nmx[:, q, k:k + 1], scale=scale, accum_out=rsum[:, q, k:k + 1])
                    i.then_inc(exp_ok, 1)

                def outs(u):
                    g, q = g0 + u, u % 2
                    act.wait_ge(pt_ps, g + 1)
                    A_(PTb[q], bank(4 + q, TT, T), ACT.Copy).then_inc(pt_ev, 1)
                    act.wait_ge(o2_ps, g + 1)
                    if u < 8:
                        r = 64 * (u % 2)
                        A_(cat[r:r + 64, u // 2, :], bank(6 + q, T)[r:r + 64, :], ACT.Copy).then_inc(o2_ev, 1)
                    elif u < 12:
                        A_(ot[:, :, (u - 8) * 64:(u - 8) * 64 + 64], bank(6 + q, TT, 64), ACT.Copy).then_inc(o2_ev, 1)
                    else:
                        A_(cat2[:, 2 * (u - 12):2 * (u - 12) + 2, :], bank(6 + q, TT, T), ACT.Copy).then_inc(o2_ev, 1)

                def attention(units):
                    exps(units[0])
                    for u in units:
                        if u + 1 in units:
                            exps(u + 1)
                        outs(u)

                attention(range(12))
                act.wait_ge(ln_ok, 2 * l + 2)
                root(st8, st8, 64).then_inc(root_ok, 1)
                for k in range(2):
                    act.wait_ge(tc_ps, 2 * l + k + 1)
                    A_(cat[:, 4 + 2 * k:6 + 2 * k, :], bank(6 + k, 2, T), ACT.Copy).then_inc(cat_ok, 1)
                evac_squares(yb)

                def evac_km(chunks):
                    for j in chunks:
                        b = take()
                        evac(km[:, j, :], bank(b, T))

                evac_km(range(4))
                norm_root()
                evac_km(range(4, 6))
                squares(sq, xT[:, :, :], n0 + 3)
                evac_km(range(6, 8))
                norm_root()
                for j in range(4):
                    b = take()
                    evac(vm[:, :, j * T:j * T + T], bank(b, TT, T))
                for j in range(8):
                    b = take()
                    evac(qm[:, j, :], bank(b, T))
                attention(range(12, 16))
                evac_squares(yb2)
                norm_root()
                squares(sq, xT[:, :, :], n0 + 5)
                norm_root()
                for i in range(FFN_PAIRS):
                    f = FFN_PAIRS * l + i
                    q = f % 2
                    act.wait_ge(up_ps, f + 1)
                    for k in range(4):
                        ch = 2 * i + k % 2 + 22 * (k // 2)
                        a = A_(ca[:, q, k, :], bank(2 * q + k // 2, 2, T)[:, k % 2, :], ACT.Identity,
                               bias=PR(f"fbias{l}")[:, ch:ch + 1], scale=PR(f"fconv{l}", 3, 44)[:, 1, ch:ch + 1])
                    a.then_inc(tap_ok, 1)
                    act.wait_ge(conv2_ok, f + 1)
                    A_(ca[:, q, 0:2, :], ca[:, q, 0:2, :], ACT.Gelu_apprx_tanh).then_inc(gelu_ok, 1)
                act.wait_ge(ffn_ps, l + 1)
                A_(yb, bank(4, KC, T), ACT.Copy).then_inc(y_ok, 1)
                act.wait_ge(y_ok, l + 1)
                squares(sq, yb)
                norm_root()
            act.wait_ge(h_ok, 3 + 7 * LAYERS)
            act.dma_start(out_d, xT[:, :, :]).then_inc(out_done, 16)
            act.wait_ge(out_done, 16)

        @block.vector
        def _(dve):
            V = nc.vector
            link = new_step(dve, v_step)
            signal = new_signal(dve)
            MUL, ADD, SUB, MAX = ALU.mult, ALU.add, ALU.subtract, ALU.max

            def tt(out, a, b, op=MUL):
                return V.tensor_tensor(out, a, b, op)

            def ts(out, a, s1, op0, s2=None, op1=None):
                return V.tensor_scalar(out, a, s1, s2, op0, op1) if op1 is not None else V.tensor_scalar(out, a, s1, None, op0)

            def stt(out, a, s1, b, op0=MUL, op1=ADD):
                return V.scalar_tensor_tensor(out, a, s1, b, op0, op1)

            roots = [0]

            def rstd(v):
                roots[0] += 1
                dve.wait_ge(root_ok, roots[0])
                link(V.reciprocal(v, v))

            V.memset(silu_c, 0.0).then_inc(silu_0, 1)
            dve.wait_ge(ld_par, 16)
            dve.wait_ge(ld_cst, 32)
            dve.wait_ge(ld_x, 48)
            link(V.tensor_copy(posf, ipos[:, :]))
            link(tt(ang, over(posf, [P, TT, N_FREQ], 2), over(C("invf"), [P, TT, N_FREQ])))
            magic = 1.5 * 2.0 ** 23
            link(ts(angk, ang, 0.15915494309189535, MUL, magic, ADD))
            link(ts(angk, angk, magic, SUB))
            for part in (6.28125, 0.0019350051879882812, 3.0199158e-07):
                link(stt(ang, angk, -part, ang))
            pi = 3.1415925
            link(ts(angk, ang, pi, ALU.min, -pi, MAX))
            link(ts(ang, ang, 1.5707963267948966, ADD))
            link(ts(cosx, ang, pi, ALU.is_gt, -6.283185307179586, MUL))
            link(tt(ang, ang, cosx, ADD))
            signal(ts(ang, ang, pi, ALU.min, -pi, MAX), rope_v)
            for l in range(LAYERS):
                v = RW(f"lam{l}", 2, 2, 32)
                link(tt(lam_p, v[:, :, 0, :], v[:, :, 1, :]))
                link(V.tensor_reduce(lam_s[:, 2 * l:2 * l + 2], lam_p, axis=AX.X, op=ADD))
            signal(ts(nmx[:, 0, :], lam_s, 0.0, ADD), rope_v)
            dve.wait_ge(rope_a, 2)
            for l in range(LAYERS):
                init = 0.8 - 0.6 * 2.718281828459045 ** (-0.3 * l)
                link(tt(nlam[:, l:l + 1], lam_s[:, 2 * l + 1:2 * l + 2], lam_s[:, 2 * l:2 * l + 1], SUB))
                link(ts(nlam[:, l:l + 1], nlam[:, l:l + 1], -init, ADD))

            norms = [0]
            rstd(rsA)
            link(tt(sqA[:, :, 0:T], ctxT, over(rsA[:, 0:T], [P, KC, T])))
            link(tt(sqA[:, :, T:2 * T], xT[:, :, :], over(rsA[:, T:2 * T], [P, KC, T])))
            with dve.Fori(0, S_MOD // SLOTS) as r:
                for k in range(SLOTS // 4):
                    at = r * (2 * SLOTS) + 8 * k
                    dve.wait_ge(modt_ps, r * 3 + k + 1)
                    tt(mods[:, bass.ds(at, 8), :].rearrange("p (q h) v -> p h q v", h=2),
                       bank(5, 2, 4, 32)[:, :, :, 0:2],
                       PR("bmod")[:, bass.ds(at, 8)].rearrange("p (q h) -> p h q", h=2).unsqueeze(3)
                       .to_broadcast([P, 2, 4, 2]), ADD).then_inc(mods_ok, 1)
            dve.wait_ge(mods_ok, 6)
            link(stt(mulx, mods[:, KC:2 * KC, 0], 1.0, PR("norm1"), ADD, MUL))
            link(stt(mulc, mods[:, KC:2 * KC, 1], 1.0, PR("norm1"), ADD, MUL))
            link(stt(mul2, mods[:, 4 * KC:5 * KC, 0], 1.0, PR("norm2"), ADD, MUL))
            for c in range(KC):
                ts(hA[:, c, 0:T], sqA[:, c, 0:T], mulc[:, c:c + 1], MUL, mods[:, c, 1:2], ADD)
                i = ts(hA[:, c, T:2 * T], sqA[:, c, T:2 * T], mulx[:, c:c + 1], MUL, mods[:, c, 0:1], ADD)
            signal(i, h_ok)

            dve.wait_ge(proj_ev, 1)
            link(tt(gtmp, graw[:, :, 8:16], over(RW("dtb"), [P, 4, 8]), ADD))
            signal(stt(gtmp2, gtmp, -1.0, gtmp, MUL, MAX), gate_v)
            dve.wait_ge(gate_a, 2)
            link(stt(gtmp, gtmp, 0.0, gtmp2, MAX, ADD))
            link(ts(gtmp, gtmp, -1.0, MUL))
            signal(tt(gt.rearrange("p d t h -> p t d h"), gtmp.rearrange("p t (d h) -> p t d h", d=2),
                      nega.rearrange("p (d h) -> p d h", d=2).unsqueeze(1).to_broadcast([P, 4, 2, H1])), gate_v)

            cw = PR("conv", 9, 12)
            dve.wait_ge(zeroed, 1)
            for j in range(12):
                dve.wait_ge(proj_ev, 5 + j + 1)
                g = padx[:, j, :].rearrange("p (r c) -> p r c", c=PW)
                dst = qT[:, j, :] if j < 4 else (kT[:, j - 4, :] if j < 8 else vT[:, j - 8, :])
                dx = (dst if j < 4 else dst[:, T:2 * T]).rearrange("p (r c) -> p r c", c=GRID_W)
                taps = [4, 0, 1, 2, 3, 5, 6, 7, 8]
                for n, k in enumerate(taps):
                    src = g[:, k // 3:k // 3 + GRID_R, k % 3:k % 3 + GRID_W]
                    w = cw[:, k, j:j + 1]
                    ins = [ts(dx, src, w, MUL) if n == 0 else stt(dx, src, w, dx)]
                    if j >= 4 and n < 3:
                        k1 = [4, 3, 5][n]
                        src = padc[:, j - 4, k1 - 3:k1 - 3 + T]
                        w = cw[:, k1, j:j + 1]
                        ins.append(ts(dst[:, 0:T], src, w, MUL) if n == 0 else stt(dst[:, 0:T], src, w, dst[:, 0:T]))
                    if n < 8:
                        link(ins[-1])
                    else:
                        ins[-1].then_inc(conv_ok, 1)

            rstd(rsk)
            rstd(rsq)
            link(stt(qT, qT, float(P) ** -0.5, rsq, MUL, MUL))
            signal(tt(kT, kT, rsk), l2_ok)
            dve.wait_ge(gate_ps, 1)
            link(V.tensor_copy(gc.rearrange("p d t h -> p (d t h)"), bank(6, 64)[:, 0:32]))
            link(V.tensor_copy(et.rearrange("p d t h -> p (d t h)"), bank(6, 64)[:, 32:64]))
            signal(tt(ed, et, gc, SUB), gate_v)
            dve.wait_ge(gate_a, 3)
            signal(tt(beg, beta, eg), gdn_start)
            for d in range(2):
                signal(V.memset(bS[:, d], 0.0), gdn["S"])

            for s in range(4):
                tiles = (s, s ^ 1)
                xs = s >= 2
                full_h = [P, H1, P]

                def per_head(v, d):
                    return over(v[:, d, tiles[d], :], full_h, 2)

                for d in range(2):
                    dve.wait_ge(gdn["gb"], 2 * s + d + 1)
                    dve.wait_ge(gdn["neg"], 2 * s + d + 1)
                    tt(bC[:, d], bank(d, H1, P), bC[:, d], ADD).then_inc(gdn["pre"], 1)
                for d in range(2):
                    dve.wait_ge(gdn["kk"], 2 * s + d + 1)
                    dve.wait_ge(gdn["exp"], 2 * s + d + 1)
                    link(tt(bM[:, d], bank(4 + d, H1, P), bC[:, d]))
                    if xs:
                        link(tt(bA[:, d], bank(6 + d, H1, P), bC[:, d]))
                        dve.wait_ge(gdn["eq"], 2 * (s - 2) + d + 1)
                        tq = (tiles[d] - 2) * P
                        link(tt(bQ[:, d], bQ[:, d], qT[:, :, tq:tq + P]))
                    link(tt(bM[:, d], bM[:, d], bank(2 + d, H1, P)))
                    signal(tt(bC[:, d], bM[:, d], over(C(f"lev{d}", 7, P)[:, 0, :], full_h)), gdn["ct"])
                for d in range(2):
                    link(tt(bT[:, d], bC[:, d], over(ident, full_h), ADD))
                    dve.wait_ge(gdn["u"], 14 * s + d + 1)
                    signal(tt(bD[:, d], bank(d, H1, P), over(ident, full_h), ADD), gdn["d"])
                for v in range(1, len(LEVELS)):
                    for d in range(2):
                        if v < len(LEVELS) - 1:
                            dve.wait_ge(gdn["dd"], 10 * s + 2 * (v - 1) + d + 1)
                            signal(tt(bD[:, d], bD[:, d], bank(2 + d, H1, P), ADD), gdn["dn"])
                        dve.wait_ge(gdn["vv"], 12 * s + 2 * (v - 1) + d + 1)
                        signal(tt(bT[:, d], bT[:, d], bank(4 + d, H1, P), ADD), gdn["d"])
                for d in range(2):
                    dve.wait_ge(gdn["tr"], 2 * s + d + 1)
                    link(tt(bM[:, d], bank(d, H1, P), per_head(beg, d)))
                    link(tt(bC[:, d], bank(d, H1, P), per_head(ed, d)))
                    signal(tt(bD[:, d], bank(6 + d, H1, P), per_head(beta, d)), gdn["tok"])
                for d in range(2):
                    dve.wait_ge(gdn["st"], 2 * s + d + 1)
                    if xs:
                        tq = (tiles[d] - 2) * P
                        o = oT[:, :, tq:tq + P]
                        if s == 2:
                            link(V.tensor_copy(o, bank(6 + d, H1, P)))
                        else:
                            link(tt(o, o, bank(6 + d, H1, P), ADD))
                    link(tt(bS[:, d], bS[:, d], per_head(et, d)))
                    signal(tt(bS[:, d], bS[:, d], bank(d, H1, P), ADD), gdn["S"])

            rstd(rso)
            link(tt(oT, oT, rso))
            signal(stt(oT, oT, PR("onorm"), zT, MUL, MUL), o_ok)
            for c in range(KC):
                dve.wait_ge(proj_ev, 21 + c + 1)
                i = stt(xT[:, c, :], yb[:, c, :], mods[:, 2 * KC + c, 0:1], xT[:, c, :])
            signal(i, x_ok)

            def pre_norm(dst, g, b=None, src=xT, n=KC):
                rstd(rs[:, 0:T])
                if b is not None:
                    link(tt(sq, src[:, :, :], over(rs[:, 0:T], [P, KC, T])))
                for c in range(KC):
                    i = stt(dst[:, c, :], src[:, c, :], g[:, c:c + 1], rs[:, 0:T], MUL, MUL) if b is None else \
                        ts(dst[:, c, :], sq[:, c, :], g[:, c:c + 1], MUL, b(c), ADD)
                signal(i, h_ok)

            def post_norm(g, y=yb):
                rstd(rs[:, 0:T])
                link(tt(y, y, over(rs[:, 0:T], [P, KC, T])))
                for c in range(KC):
                    i = stt(xT[:, c, :], y[:, c, :], g[:, c:c + 1], xT[:, c, :])
                signal(i, h_ok)

            pre_norm(h2, mul2, lambda c: mods[:, 3 * KC + c, 0:1])
            rstd(rs[:, T:2 * T])
            link(tt(memN, memN, over(rs[:, T:2 * T], [P, KC, T])))
            link(V.memset(zeros, 0.0))

            dve.wait_ge(proj_ev, 30)
            m, den, m1, m2, w1, w2, dd = r1v[:, 0], r1v[:, 1], r1v[:, 3], r1v[:, 4], r1v[:, 5], r1v[:, 6], r1v[:, 2]
            lg, le = logits[:, :, 0:4], logits[:, :, 4:36]
            link(tt(lg, lg, over(RW("bgroup"), [P, TT, 4]), ADD))
            link(tt(le, le, over(RW("brouter"), [P, TT, 32]), ADD))

            def col(v, n):
                return over(v, [P, TT, n], 2)

            def first_max(onehot, mxv, src, tmp, first, n):
                link(V.tensor_reduce(mxv, src, axis=AX.X, op=MAX))
                link(tt(tmp, src, col(mxv, n), ALU.is_ge))
                link(tt(tmp, tmp, over(C(first), [P, TT, n])))
                link(V.tensor_reduce(den, tmp, axis=AX.X, op=MAX))
                link(tt(onehot, tmp, col(den, n), ALU.is_equal))

            first_max(r4b, m, lg, r4a, "first4", 4)
            link(tt(r4a, lg, col(m, 4), SUB))
            link(tt(elp.rearrange("p t (g e) -> p t g e", g=4), le.rearrange("p t (g e) -> p t g e", g=4),
                    r4b.unsqueeze(3).to_broadcast([P, TT, 4, 8])))
            link(V.tensor_reduce(r8a, elp.rearrange("p t (g e) -> p t e g", g=4), axis=AX.X, op=ADD))
            first_max(r8b, m1, r8a, r8c, "first8", 8)
            link(stt(r8a, r8b, NEG, r8a))
            first_max(r8c, m2, r8a, r8c, "first8", 8)
            signal(tt(dd, m2, m1, SUB), rt_v)
            link(tt(r8a, r8b, r8c, ADD))
            for t in range(TT):
                i = tt(routed[:, t, :].rearrange("p (g e) -> p g e", g=4), over(r4b[:, t, :], [P, 4, 8], 2),
                       over(r8a[:, t, :], [P, 4, 8]))
            signal(i, zeros_ok)
            dve.wait_ge(rt_a, 1)
            link(V.tensor_reduce(den, r4a, axis=AX.X, op=ADD))
            link(ts(w1, dd, 1.0, ADD))
            link(tt(w1, w1, den))
            link(V.reciprocal(w1, w1))
            link(tt(w2, w1, dd))
            link(tt(r8b, r8b, col(w1, 8)))
            link(tt(r8c, r8c, col(w2, 8)))
            link(tt(r8b, r8b, r8c, ADD))
            for t in range(TT):
                link(tt(comb[:, t, :].rearrange("p (g e) -> p g e", g=4), over(r4b[:, t, :], [P, 4, 8], 2),
                        over(r8b[:, t, :], [P, 4, 8])))
            dve.wait_ge(rank_ps, 1)
            link(tt(rank, bank(6, 96)[:, 0:64].rearrange("p (t e) -> p t e", t=TT), routed))
            link(ts(rank, rank, -1.0, ADD))
            link(V.tensor_reduce(load[:, 0:1], bank(6, 96)[:, 64:96], axis=AX.X, op=MAX))
            for k in range(1, T // SLOTN):
                i = ts(rounds_f[:, k:k + 1], load[:, 0:1], float(SLOTN * k), ALU.is_gt)
            link(i)
            link(V.tensor_reduce(rounds_f[:, 0:1], rounds_f[:, 1:4], axis=AX.X, op=ADD))
            link(ts(rounds_f[:, 0:1], rounds_f[:, 0:1], 1.0, ADD))
            signal(V.tensor_copy(rounds_i[:, :], rounds_f[:, 0:1]), rounds_ok)
            rounds = dve.value_load(rounds_i[0:1, 0:1], min_val=1, max_val=T // SLOTN)
            with dve.Fori(0, rounds) as r:
                with dve.Fori(0, PAIRS) as i:
                    def at(k, c):
                        return r * (PAIRS * k) + i * k + c

                    def pair(v):
                        return v[:, :, bass.ds(i * 2, 2)].unsqueeze(3).to_broadcast([P, TT, 2, SLOTN])

                    iota = C("iota").unsqueeze(1).unsqueeze(1).to_broadcast([P, TT, 2, SLOTN])
                    tt(sel, iota, pair(rank), ALU.is_equal).then_inc(sel_ok, 1)
                    dve.wait_ge(sel_ok, at(1, 1))
                    tt(selw, sel, pair(comb)).then_inc(swt_ok, 1)
                    dve.wait_ge(sg_ok, at(1, 1))
                    tt(hid, sg, bank(3, 512)).then_inc(hid_ok, 1)
                    dve.wait_ge(tr_ps, at(1, 1))
                    V.tensor_copy(selT, bank(1, T)).then_inc(selT_ok, 1)
                    dve.wait_ge(y_ps, at(2, 2))
                    V.tensor_copy(ytok[:, 4:8, :], bank(3, 4, P)).then_inc(yhigh_ok, 1)
                ts(rank, rank, -float(SLOTN), ADD).then_inc(rank_dn, 1)
                dve.wait_ge(rank_dn, r + 1)
            dve.wait_ge(moe_ps, 2)
            for c in range(KC):
                i = stt(xT[:, c, :], bank(4 + c // 2, 2, T)[:, c % 2, :], mods[:, 5 * KC + c, 0:1], xT[:, c, :])
            signal(i, x_ok)
            pre_norm(xT, PR("final"))

            for l in range(LAYERS):
                n0 = 3 + 7 * l
                g0 = 16 * l
                e0 = 30 + 55 * l
                pre_norm(h, PR(f"mix_pre{l}"))
                rstd(rs)
                for c in range(5):
                    g = PR(f"cq{l}")[:, c:c + 1] if c < 3 else PR(f"ckv{l}")[:, c - 3:c - 2]
                    i = stt(cv[:, c, :], cv[:, c, :], g, rs[:, 0:T] if c < 3 else rs[:, T:2 * T], MUL, MUL)
                signal(i, h_ok)
                dve.wait_ge(proj_ev, e0 + 8)
                vv = zt[:, :, 256:512].rearrange("p t (g c) -> p t g c", g=4)
                s8 = [P, TT, 4, 64]
                st, stb = [x.rearrange("p (t g) -> p t g", t=TT) for x in (st8, st8b)]
                tmp = A(16704, TT, 4, 64)
                link(V.tensor_reduce(st, vv, axis=AX.X, op=ADD))
                link(ts(st8, st8, 1.0 / 64, MUL))
                link(tt(vv, vv, st.unsqueeze(3).to_broadcast(s8), SUB))
                link(tt(tmp, vv, vv))
                signal(V.tensor_reduce(stb, tmp, axis=AX.X, op=ADD), ln_ok)
                rstd(st8b)
                link(tt(vv, vv, stb.unsqueeze(3).to_broadcast(s8)))
                link(tt(zt[:, :, 256:512], zt[:, :, 256:512], over(RW(f"sgu_g{l}"), [P, TT, 256])))

                def rotate(x1, x2, c, s, o1, o2, t, put=None):
                    tt(t[0], x1, c)
                    tt(t[1], x2, s)
                    tt(t[2], x2, c)
                    link(tt(t[3], x1, s))
                    put = put or (lambda v: v)
                    tt(o1, put(t[0]), put(t[1]), SUB)
                    return tt(o2, put(t[2]), put(t[3]), ADD)

                def table(v, lo, n, k):
                    return v[:, :, lo:lo + n].unsqueeze(2).to_broadcast([P, TT, k, n])

                dve.wait_ge(proj_ev, e0 + 15)
                qv = qt.rearrange("p t (h d) -> p t h d", d=MLA_D)
                kv = kc.rearrange("p t (h d) -> p t h d", d=MLA_D)
                t8 = [rtmp[:, k].rearrange("p (t h d) -> p t h d", t=TT, h=8) for k in range(4)]
                i = rotate(qv[:, :, :, 64:80], qv[:, :, :, 80:96], table(cosx, 0, 16, 8), table(sinx, 0, 16, 8),
                           qv[:, :, :, 64:80], qv[:, :, :, 80:96], t8)
                signal(i, qk_ok)
                dve.wait_ge(proj_ev, e0 + 19)
                tk = [rtk[:, k].rearrange("p (t d) -> p t d", t=TT) for k in range(4)]
                i = rotate(krt[:, :, 0:16], krt[:, :, 16:32], cosx[:, :, 0:16], sinx[:, :, 0:16],
                           kv[:, :, :, 64:80], kv[:, :, :, 80:96], tk,
                           lambda v: v.unsqueeze(2).to_broadcast([P, TT, 8, 16]))
                signal(i, qk_ok)
                dv = dt_[:, :, 0:512].rearrange("p t (u d) -> p t u d", d=32)
                t16 = [rtmp[:, k].rearrange("p (t h d) -> p t h d", t=TT, h=16) for k in range(4)]
                i = rotate(dv[:, :, :, 0:8], dv[:, :, :, 8:16], table(cosx, 16, 8, 16), table(sinx, 16, 8, 16),
                           dv[:, :, :, 0:8], dv[:, :, :, 8:16], t16)
                signal(i, qk_ok)

                def maxima(u):
                    g, q = g0 + u, u % 2
                    dve.wait_ge(sc_ps, g + 1)
                    n = 4 if 8 <= u < 12 else 2
                    scale = (MLA_D if u < 8 else 32 if u < 12 else 256) ** -0.5
                    link(V.tensor_reduce(mx[:, q, 0:n], bank(2 * q, n, T), axis=AX.X, op=MAX))
                    signal(ts(nmx[:, q, 0:n], mx[:, q, 0:n], -scale, MUL), max_ok, False)

                def normalize(u):
                    g, q = g0 + u, u % 2
                    dve.wait_ge(exp_ok, g + 1)
                    n = 4 if 8 <= u < 12 else 2
                    link(V.reciprocal(rinv[:, q, 0:n], rsum[:, q, 0:n]))
                    if n == 2:
                        for t in range(TT):
                            i = ts(Pb[q][:, t, :], Pb[q][:, t, :], rinv[:, q, t:t + 1], MUL)
                    else:
                        link(ts(rinv[:, q, 2:4], rinv[:, q, 2:4], nlam[:, l:l + 1], MUL))
                        for t in range(TT):
                            i = ts(Pb[2 + q][:, t, :], Pb[2 + q][:, t, :], rinv[:, q, 2 + t:3 + t], MUL)
                        link(i)
                        for t in range(TT):
                            i = stt(Pb[q][:, t, :], Pb[q][:, t, :], rinv[:, q, t:t + 1], Pb[2 + q][:, t, :])
                    i.then_inc(p_ok, 1)

                def attention(units):
                    maxima(units[0])
                    for u in units:
                        if u + 1 in units:
                            maxima(u + 1)
                        normalize(u)

                attention(range(12))
                dve.wait_ge(mix_ps, l + 1)
                mixv = bank(4, TT * 4, 64)
                obv = ob.rearrange("p t (g c) -> p (t g) c", g=4)
                for t in range(TT):
                    i = tt(obv[:, 4 * t:4 * t + 4, :], mixv[:, 4 * t:4 * t + 4, :], over(PR(f"sgu_b{l}"), [P, 4, 64], 2), ADD)
                link(i)
                signal(tt(ob, ob, zt[:, :, 0:256]), ot_ok)
                dve.wait_ge(o2_ev, g0 + 12)
                otv = ot.rearrange("p t (h c) -> p t h c", h=4)
                link(tt(tmp, otv, otv))
                signal(V.tensor_reduce(st, tmp, axis=AX.X, op=ADD), ln_ok)
                rstd(st8)
                link(ts(st8, st8, 1.0 - (0.8 - 0.6 * 2.718281828459045 ** (-0.3 * l)), MUL))
                link(tt(otv, otv, st.unsqueeze(3).to_broadcast(s8)))
                signal(tt(ot.rearrange("p t (h c) -> p (t h) c", h=4), ot.rearrange("p t (h c) -> p (t h) c", h=4),
                          over(RW(f"sub_g{l}"), [P, TT * 4, 64])), ot_ok)
                g = PR(f"mem_kv{l}")
                for c in range(KC):
                    i = ts(memn[:, c, :], memN[:, c, :], g[:, c:c + 1], MUL)
                i.then_inc(memn_ok, 1)
                post_norm(PR(f"mix_post{l}"))
                pre_norm(h, PR(f"mem_pre{l}"))
                attention(range(12, 16))
                post_norm(PR(f"mem_post{l}"), yb2)
                pre_norm(h, PR(f"ffn_pre{l}"))
                fw = PR(f"fconv{l}", 3, 44)
                for i_ in range(FFN_PAIRS):
                    f = FFN_PAIRS * l + i_
                    q = f % 2
                    dve.wait_ge(tap_ok, f + 1)
                    for side in range(2):
                        for k in range(4):
                            ch = 2 * i_ + k % 2 + 22 * (k // 2)
                            src = bank(2 * q + k // 2, 2, T)[:, k % 2, :]
                            dst = ca[:, q, k, 1:T] if side == 0 else ca[:, q, k, 0:T - 1]
                            src = src[:, 0:T - 1] if side == 0 else src[:, 1:T]
                            i = stt(dst, src, fw[:, 2 * side, ch:ch + 1], dst)
                        if side == 0:
                            link(i)
                    signal(i, conv2_ok, False)
                    dve.wait_ge(gelu_ok, f + 1)
                    dve.wait_ge(conv2_ok, f + 1)
                    tt(fT[:, q], ca[:, q, 0:2, :], ca[:, q, 2:4, :]).then_inc(f_ok, 1)
                post_norm(PR(f"ffn_post{l}"))


def rows_of(v, k):
    return v.reshape(-1, k, 128).transpose(2, 0, 1).reshape(128, -1)


def tiles(w, n):
    k, m = w.shape
    return w.reshape(k // 128, 128, m // n, n).transpose(2, 1, 0, 3).reshape(m // n, 128, -1)


def kernel(**inputs):
    import numpy as np
    import concourse.bacc as bacc
    from concourse.bass_utils import run_bass_kernel_spmd

    a = {k: np.asarray(v) for k, v in inputs.items()}
    stream = np.zeros((S_ALL, P, SLOT), np.float32)
    at = [0]

    def put(t):
        stream[at[0]:at[0] + t.shape[0], :, :t.shape[2]] = t
        at[0] += t.shape[0]

    put(tiles(a["w_mod"][0], 256))
    w_in = a["w_in"][0]
    put(tiles(w_in[:, :2560], 256))
    put(tiles(a["w_out"][0], 256))
    for i in range(PAIRS):
        pair = slice(2 * i, 2 * i + 2)
        g, u = [np.stack([tiles(w, 256) for w in a[n][0, pair]], 1) for n in ("w_gate", "w_up")]
        put(np.stack([g, u], 1).reshape(8, P, SLOT))
        put(np.stack([tiles(w, 512) for w in a["w_down"][0, pair]], 1).reshape(4, P, SLOT))
    for l in range(LAYERS):
        w = a["w_in_2"][l]
        wp = np.zeros((D, 2048), np.float32)
        wp[:, :672] = w[:, :672]
        wp[:, 768:] = w[:, 672:]
        put(tiles(wp, 256))
        put(tiles(a["mla_w_uq_2"][l], 384))
        put(tiles(a["mla_w_ukv_2"][l], 1024))
        put(tiles(a["w_mix_out_2"][l], 256))
        put(tiles(a["mem_w_kv_2"][l], 256))
        put(tiles(a["mem_w_q_2"][l], 256))
        put(tiles(a["mem_w_o_2"][l], 256))
        up, down = tiles(a["ffn_w_up_2"][l], 256), a["ffn_w_down_2"][l]
        down = down.reshape(FFN_PAIRS, 2, P, D).transpose(0, 2, 1, 3).reshape(FFN_PAIRS, P, 2 * D)
        for i in range(FFN_PAIRS):
            put(np.stack([up[i], up[FFN_PAIRS + i]]))
            if i:
                put(down[i - 1:i])
        put(down[FFN_PAIRS - 1:])
    assert at[0] == S_ALL

    par = np.zeros((P, N_PAR), np.float32)
    row = np.zeros((P, N_ROW), np.float32)

    def set_par(name, v):
        o, n = PAR[name]
        par[:, o:o + n] = v

    def set_row(name, v):
        o, n = ROW[name]
        row[:, o:o + n] = v.reshape(1, n)

    set_par("norm1", rows_of(a["norm1_g"], 8))
    set_par("norm2", rows_of(a["norm2_g"], 8))
    set_par("final", rows_of(a["final_g"], 8))
    set_par("bmod", rows_of(a["b_mod"], 48))
    set_par("c", np.stack([rows_of(a["c"], 8), rows_of(a["c_ctx"], 8)], 2).reshape(P, 16))
    set_par("conv", rows_of(a["conv_w"][0].reshape(9, 1536), 12))
    set_par("onorm", a["onorm_g"].reshape(P, 1))
    set_par("wgates", tiles(np.ascontiguousarray(w_in[:, 2560:]), 16)[0])
    set_par("wroute", tiles(np.concatenate([a["w_group"][0], a["w_router"][0]], 1), 36)[0])
    set_row("alog", a["a_log"])
    set_row("dtb", a["dt_bias"])
    set_row("bgroup", a["b_group"])
    set_row("brouter", a["b_router"])
    names = [("mix_pre", "mix_pre_g_2", 8), ("mix_post", "mix_post_g_2", 8), ("cq", "mla_cq_g_2", 3),
             ("ckv", "mla_ckv_g_2", 2), ("mem_pre", "mem_pre_g_2", 8), ("mem_post", "mem_post_g_2", 8),
             ("mem_kv", "mem_kv_g_2", 8), ("ffn_pre", "ffn_pre_g_2", 8), ("ffn_post", "ffn_post_g_2", 8),
             ("fconv", "ffn_conv_w_2", 44), ("fbias", "ffn_conv_b_2", 44)]
    for l in range(LAYERS):
        for name, key, k in names:
            set_par(f"{name}{l}", rows_of(a[key][l], k))
        set_par(f"sgu_b{l}", a["sgu_b_s_2"][l].T)
        set_row(f"sgu_g{l}", a["sgu_norm_g_2"][l])
        set_row(f"sub_g{l}", a["diff_sub_g_2"][l])
        set_row(f"lam{l}", np.concatenate([a[f"diff_lam_{n}_2"][l] for n in ("q1", "k1", "q2", "k2")]))

    def chan(v):
        return v.T.reshape(KC, P, T).transpose(1, 0, 2)

    cst, dft = constants()
    arrays = {
        "stream": stream, "par": par, "row": row, "cst": cst, "dft": dft,
        "xc": np.stack([chan(a["ctx"][0]), chan(a["x"][0])]),
        "mem": chan(a["mem_2"][0]),
        "pos": a["positions_2"].reshape(TT, P).T,
        "sguw": a["sgu_w_s_2"].transpose(0, 3, 1, 2),
    }
    nc = bacc.Bacc("TRN2", target_bir_lowering=False, num_devices=1)
    args = []
    arrays = {"in_" + k: np.ascontiguousarray(v) for k, v in arrays.items()}
    for k, v in arrays.items():
        args.append(nc.dram_tensor(k, v.shape, mybir.dt.from_np(v.dtype), kind="ExternalInput").ap())
    out = nc.dram_tensor("out_y", (P, KC, T), F32, kind="ExternalOutput").ap()
    trunk_kernel(nc, *args, out)
    r = run_bass_kernel_spmd(nc, [arrays], core_ids=[0])
    y = np.asarray(r.results[0]["out_y"])
    return np.ascontiguousarray(y.transpose(1, 0, 2).reshape(D, T).T).reshape(1, T, D)
```
